# Optimizing a Trainium2 kernel written in Bass

```python
import math
import jax, jax.numpy as jnp
from jax import lax
import numpy as np

D_MODEL = 1024
BATCH = 1
SEQ = 512
DEPTH = 1

HG_HEADS = 4
HG_DIM = 128
HG_WIDTH = HG_HEADS * HG_DIM
HG_CHUNK = 64
AT_HEADS = 8
AT_KV_GROUPS = 2
AT_HEAD_DIM = 64
AT_WIDTH = AT_HEADS * AT_HEAD_DIM
AT_KV_WIDTH = AT_KV_GROUPS * AT_HEAD_DIM
Q_LORA = 256
IDX_HEADS = 8
IDX_DIM = 64
TOPK_MAX = 256
Q_BLOCK = 128
REL_BUCKETS = 32
REL_MAX_DIST = 128
D_FF = 4 * D_MODEL
EPS = 1e-6

IN_WIDTHS = (HG_WIDTH, HG_WIDTH, HG_WIDTH, HG_WIDTH,
             Q_LORA, AT_KV_WIDTH, AT_KV_WIDTH,
             IDX_DIM, IDX_HEADS,
             D_MODEL, D_MODEL)
IN_COLS = sum(IN_WIDTHS)

kernel_name = "hybrid_hgrn2_dsa_gated_block"

def _split_points():
    pts, acc = [], 0
    for w in IN_WIDTHS[:-1]:
        acc += w
        pts.append(acc)
    return tuple(pts)

def rms_norm(x, g):
    xf = x.astype(jnp.float32)
    y = xf * lax.rsqrt(jnp.mean(xf * xf, axis=-1, keepdims=True) + EPS)
    return (y * g.astype(jnp.float32)).astype(x.dtype)

def layer_norm(x, g, b):
    xf = x.astype(jnp.float32)
    mu = jnp.mean(xf, axis=-1, keepdims=True)
    var = jnp.mean(jnp.square(xf - mu), axis=-1, keepdims=True)
    y = (xf - mu) * lax.rsqrt(var + EPS)
    return (y * g.astype(jnp.float32) + b.astype(jnp.float32)).astype(x.dtype)

def hgrn2_lower_bounds(lb_logits):
    p = jax.nn.softmax(lb_logits.astype(jnp.float32), axis=0)
    return jnp.cumsum(p, axis=0)

def hgrn2_mixer(q, f_logit, i, lb):
    B, T, _ = q.shape
    C = HG_CHUNK
    n = T // C
    f = lb + (1.0 - lb) * jax.nn.sigmoid(f_logit.astype(jnp.float32))
    log_f = jnp.log(f)
    k = 1.0 - f

    def to_chunks(a):
        return a.astype(jnp.float32).reshape(B, n, C, HG_HEADS, HG_DIM).transpose(1, 0, 3, 2, 4)

    qc, kc, vc, gc = to_chunks(q), to_chunks(k), to_chunks(i), to_chunks(log_f)
    causal = jnp.tril(jnp.ones((C, C), dtype=bool))[:, :, None]

    def step(S, inp):
        qt, kt, vt, gt = inp
        b = jnp.cumsum(gt, axis=2)
        o_inter = jnp.einsum('bhtd,bhde->bhte', qt * jnp.exp(b), S)
        diff = b[:, :, :, None, :] - b[:, :, None, :, :]
        decay = jnp.exp(jnp.where(causal, diff, -jnp.inf))
        A = jnp.einsum('bhtd,bhsd,bhtsd->bhts', qt, kt, decay)
        o = o_inter + jnp.einsum('bhts,bhse->bhte', A, vt)
        b_last = b[:, :, -1:, :]
        S = jnp.exp(b_last[:, :, 0, :])[..., None] * S + \
            jnp.einsum('bhsd,bhse->bhde', kt * jnp.exp(b_last - b), vt)
        return S, o

    S0 = jnp.zeros((B, HG_HEADS, HG_DIM, HG_DIM), jnp.float32)
    _, o = lax.scan(step, S0, (qc, kc, vc, gc))
    return o.transpose(1, 0, 3, 2, 4).reshape(B, T, HG_WIDTH)

def t5_bucket(dist):
    max_exact = REL_BUCKETS // 2
    large = max_exact + (jnp.log(jnp.maximum(dist, 1).astype(jnp.float32) / max_exact)
                         / math.log(REL_MAX_DIST / max_exact)
                         * (REL_BUCKETS - max_exact)).astype(jnp.int32)
    large = jnp.minimum(large, REL_BUCKETS - 1)
    return jnp.where(dist < max_exact, dist, large)

def dsa_mixer(q, q_idx, w_idx, k, v, k_idx, rel_bias):
    B, T, _ = q.shape
    G, R, dh = AT_KV_GROUPS, AT_HEADS // AT_KV_GROUPS, AT_HEAD_DIM
    topk = min(TOPK_MAX, T // 4)
    nb = T // Q_BLOCK
    qb_all = q.reshape(B, nb, Q_BLOCK, G, R, dh).transpose(1, 0, 2, 3, 4, 5)
    qi_all = q_idx.reshape(B, nb, Q_BLOCK, IDX_HEADS, IDX_DIM).transpose(1, 0, 2, 3, 4)
    wi_all = w_idx.reshape(B, nb, Q_BLOCK, IDX_HEADS).transpose(1, 0, 2, 3)
    pos_all = jnp.arange(T, dtype=jnp.int32).reshape(nb, Q_BLOCK)
    key_pos = jnp.arange(T, dtype=jnp.int32)
    gather = jax.vmap(lambda a, ix: a[ix])

    def block(inp):
        qb, qib, wb, tpos = inp
        rel = jax.nn.relu(jnp.einsum('bqhd,bsd->bqhs', qib, k_idx).astype(jnp.float32) * (IDX_DIM ** -0.5))
        score = jnp.einsum('bqh,bqhs->bqs', wb.astype(jnp.float32) * (IDX_HEADS ** -0.5), rel)
        causal = key_pos[None, :] <= tpos[:, None]
        score = jnp.where(causal[None], score, -jnp.inf)
        _, idx = lax.top_k(score, topk)
        kg = gather(k, idx)
        vg = gather(v, idx)
        logits = jnp.einsum('bqgrd,bqkgd->bqgrk', qb, kg).astype(jnp.float32) * (dh ** -0.5)
        dist = tpos[None, :, None] - idx
        bias = rel_bias[t5_bucket(jnp.maximum(dist, 0))]
        bias = bias.reshape(B, Q_BLOCK, topk, G, R).transpose(0, 1, 3, 4, 2).astype(jnp.float32)
        valid = (dist >= 0)[:, :, None, None, :]
        logits = jnp.where(valid, logits + bias, -jnp.inf)
        p = jax.nn.softmax(logits, axis=-1).astype(v.dtype)
        o = jnp.einsum('bqgrk,bqkgd->bqgrd', p, vg)
        return o.reshape(B, Q_BLOCK, AT_WIDTH)

    out = lax.map(block, (qb_all, qi_all, wi_all, pos_all))
    return out.transpose(1, 0, 2, 3).reshape(B, T, AT_WIDTH)

def setup_inputs(seed: int = 0) -> dict:
    key = jax.random.key(seed)
    ks = jax.random.split(key, 20)
    f32 = jnp.float32

    def w(k, shape, fan_in):
        return jax.random.normal(k, shape, f32) * (fan_in ** -0.5)

    def gain(k, shape):
        return 1.0 + 0.02 * jax.random.normal(k, shape, f32)

    return {
        "x": jax.random.normal(ks[0], (BATCH, SEQ, D_MODEL), f32),
        "attn_norm_g": gain(ks[1], (DEPTH, D_MODEL)),
        "w_in": w(ks[2], (DEPTH, D_MODEL, IN_COLS), D_MODEL),
        "hgrn_lb_logits": jax.random.normal(ks[3], (DEPTH + 1, HG_WIDTH), f32),
        "hgrn_norm_g": gain(ks[4], (DEPTH, HG_WIDTH)),
        "w_up_hgrn": w(ks[5], (DEPTH, HG_WIDTH, D_MODEL), HG_WIDTH),
        "q_norm_g": gain(ks[6], (DEPTH, Q_LORA)),
        "w_uq": w(ks[7], (DEPTH, Q_LORA, AT_WIDTH), Q_LORA),
        "w_iq": w(ks[8], (DEPTH, Q_LORA, IDX_HEADS * IDX_DIM), Q_LORA),
        "idx_k_norm_g": gain(ks[9], (DEPTH, IDX_DIM)),
        "idx_k_norm_b": 0.02 * jax.random.normal(ks[10], (DEPTH, IDX_DIM), f32),
        "rel_bias": 0.5 * jax.random.normal(ks[11], (REL_BUCKETS, AT_HEADS), f32),
        "w_up_attn": w(ks[12], (DEPTH, AT_WIDTH, D_MODEL), AT_WIDTH),
        "w_o": w(ks[13], (DEPTH, D_MODEL, D_MODEL), D_MODEL),
        "mlp_norm_g": gain(ks[14], (DEPTH, D_MODEL)),
        "w_mlp_in": w(ks[15], (DEPTH, D_MODEL, D_FF), D_MODEL),
        "w_mlp_out": w(ks[16], (DEPTH, D_FF, D_MODEL), D_FF),
        "final_norm_g": gain(ks[17], (D_MODEL,)),
    }

def reference(x, attn_norm_g, w_in, hgrn_lb_logits, hgrn_norm_g, w_up_hgrn, q_norm_g, w_uq,
              w_iq, idx_k_norm_g, idx_k_norm_b, rel_bias, w_up_attn, w_o, mlp_norm_g,
              w_mlp_in, w_mlp_out, final_norm_g):
    B, T, _ = x.shape
    splits = _split_points()
    lbs = hgrn2_lower_bounds(hgrn_lb_logits)
    for l in range(DEPTH):
        h = rms_norm(x, attn_norm_g[l])
        proj = h @ w_in[l]
        (hq, hf, hi, hg, cq, ak, av, ik, iw, gate_a, gate_b) = jnp.split(proj, splits, axis=-1)

        oa = hgrn2_mixer(hq, hf, hi, lbs[l]).astype(x.dtype)
        oa = rms_norm(oa.reshape(B, T, HG_HEADS, HG_DIM),
                      hgrn_norm_g[l].reshape(HG_HEADS, HG_DIM)).reshape(B, T, HG_WIDTH)
        oa = oa * jax.nn.silu(hg)

        cq = rms_norm(cq, q_norm_g[l])
        aq = cq @ w_uq[l]
        iq = cq @ w_iq[l]
        ik = layer_norm(ik, idx_k_norm_g[l], idx_k_norm_b[l])
        ob = dsa_mixer(aq, iq, iw,
                       ak.reshape(B, T, AT_KV_GROUPS, AT_HEAD_DIM),
                       av.reshape(B, T, AT_KV_GROUPS, AT_HEAD_DIM),
                       ik, rel_bias)

        mix = jax.nn.sigmoid(gate_a) * (oa @ w_up_hgrn[l]) + jax.nn.sigmoid(gate_b) * (ob @ w_up_attn[l])
        x = x + mix @ w_o[l]

        hm = rms_norm(x, mlp_norm_g[l])
        x = x + jnp.square(jax.nn.relu(hm @ w_mlp_in[l])) @ w_mlp_out[l]
    return rms_norm(x, final_norm_g)


_drawn_inputs = setup_inputs


def setup_inputs(seed=0):
    import zlib

    import numpy as np

    out = dict(_drawn_inputs(seed))
    spreads = {}
    factors = {'hgrn_norm_g': 8.0,
     'q_norm_g': 6.429,
     'idx_k_norm_g': 6.682,
     'idx_k_norm_b': 7.197,
     'mlp_norm_g': 3.286,
     'final_norm_g': 2.863}
    for name, (base, spread) in spreads.items():
        noise = np.random.default_rng([zlib.crc32(name.encode()), seed]).standard_normal(out[name].shape)
        drawn = base * np.exp(spread * noise) if base else spread * noise
        out[name] = __import__('jax').numpy.asarray(drawn.astype(out[name].dtype))
    for name, factor in factors.items():
        out[name] = (out[name] * factor).astype(out[name].dtype)
    return out
```

```python
from contextlib import ExitStack

import numpy as np

import concourse.bass as bass
from concourse import mybir

F32 = mybir.dt.float32
F32R = mybir.dt.float32r
I32 = mybir.dt.int32
ALU = mybir.AluOpType
ACT = mybir.ActivationFunctionType
AX = mybir.AxisListType

P = 128
T = 512
D = 1024
NT = T // P
KD_ = D // P
HG = 4
HGW = HG * P
C = P
LEVELS = 7
AH, DH = 8, 64
GR = 2
QL = 256
IH = 8
TOPK = 128
BUCKETS = 32
F = 4 * D
EPS = 1e-6
NEG = -1.0e30
FILL = -3.0e38
TAKEN = -3.4e38
SLAB = 1024
SLOTS = 4
AHEAD = 3

PLAN = ([("c0", j) for j in range(4)] + [("c1", 0)] + [("hf", j) for j in range(4)]
        + [("iq", 0), ("uq", 0)] + [("hq", j) for j in range(4)] + [("hi", j) for j in range(4)]
        + [("hg", j) for j in range(4)] + [("ga", j) for j in range(8)] + [("ua", j) for j in range(4)]
        + [("gb", j) for j in range(8)] + [("ub", j) for j in range(4)] + [("wo", j) for j in range(8)])
NPLAN = len(PLAN)
FB = 512
NFB = F // FB
PER_FB = 8
NSLAB = NPLAN + NFB * PER_FB
AT_SLAB = {k: n for n, k in reversed(list(enumerate(PLAN)))}

K_IDENT, K_MASK, K_RESET, K_CAUSAL = 0, P, P + LEVELS * 64, P + LEVELS * 64 + T
K_FLIP = K_CAUSAL + P
K_COLS = K_FLIP + P
V_ATTN, V_MLP, V_Q, V_HG, V_LB0, V_LB1, V_IKG, V_IKB = 0, 8, 16, 18, 22, 26, 30, 31
V_COLS = 32
BT_LEN = P + T


def build(nc, x, slabs, vecs, consts, onehot, rel_bias, final_g, out):
    with ExitStack() as ctx:
        at = [0]
        base = 16512

        def place(name, off_kb, cols, dt=F32, rows=P):
            return nc.alloc_sbuf_tensor_at(name, [rows, cols], dt, offset=base + int(off_kb * 1024))

        def sem(name):
            return ctx.enter_context(nc.semaphore(name))

        raw = [place(f"raw{s}", 4 * s, SLAB) for s in range(SLOTS)]
        whi = [place(f"whi{s}", 16 + 4 * s, SLAB, F32R) for s in range(SLOTS)]
        wlo = [place(f"wlo{s}", 32 + 4 * s, SLAB, F32R) for s in range(SLOTS)]
        hTh = place("hTh", 48, KD_ * T, F32R)
        hTl = place("hTl", 64, KD_ * T, F32R)
        cst = place("cst", 80, K_COLS)
        vec = place("vec", 85.25, V_COLS)
        small = place("small", 85.5, 256)
        iks = place("iks", 86.5, NT * 72)
        aq = place("aq", 88, 4 * T)
        kdup = place("kdup", 96, GR * T)
        c0s = place("c0s", 100, NT * 512)
        sc = place("sc", 108, 1280)
        hF = place("hF", 113, HG * T)
        hK = place("hK", 121, HG * T)
        hQ = place("hQ", 129, HG * T)
        hV = place("hV", 137, NT * HGW)
        hSG = place("hSG", 145, NT * HGW)
        hX = [place(f"hX{i}", 153 + 8 * i, HG * T) for i in range(2)]
        hA = place("hA", 169, HG * T)
        hS = place("hS", 177, HG * P)
        hKT = place("hKT", 179, HG * P)
        tha = place("tha", 181, KD_ * T)
        xs = place("xs", 113, NT * D)
        cqh = place("cqh", 129, 2 * T, F32R)
        cql = place("cql", 133, 2 * T, F32R)
        kd = place("kd", 137, NT * GR * P)
        ikn = place("ikn", 141, NT * P)
        iq = place("iq", 181, 4 * T)
        ikd = place("ikd", 189, T)
        rel = [place(f"rel{i}", 191 + 2 * i, T) for i in range(2)]
        rbias = place("rbias", 195, BT_LEN, rows=AH)
        oneh = place("oneh", 197.5, BT_LEN, rows=BUCKETS)
        rb = place("rb", 200, AH, rows=BUCKETS)
        hO = place("hO", 113, NT * HGW)
        oah = place("oah", 153, HG * T, F32R)
        oal = place("oal", 161, HG * T, F32R)
        bt = place("bt", 129, AH * T)
        ob = place("ob", 145, NT * 512)
        bm = [place(f"bm{i}", 169 + 2 * i, T) for i in range(2)]
        tt = [place(f"tt{i}", 173 + 2 * i, T) for i in range(2)]
        et = [place(f"et{i}", 177 + 2 * i, T) for i in range(2)]
        obh = place("obh", 113, 4 * T, F32R)
        obl = place("obl", 121, 4 * T, F32R)
        thb = place("thb", 153, KD_ * T)
        mxh = place("mxh", 88, KD_ * T, F32R)
        mxl = place("mxl", 129, KD_ * T, F32R)
        y = place("y", 153, NT * D)
        ys = place("ys", 113, NT * D)
        hh = place("hh", 169, 4 * T, F32R)
        hl = place("hl", 177, 4 * T, F32R)
        rt = [place(f"rt{i}", 185 + 2 * i, T) for i in range(2)]
        hv = [place(f"hv{i}", 189 + 2 * i, T) for i in range(2)]
        fg = place("fg", 193, D)
        junk = place("junk", 202.5, 1024)

        ssx, rsx = small[:, 0:4], small[:, 4:8]
        ssq, rsq = small[:, 8:12], small[:, 12:16]
        mv, rik = small[:, 16:24], small[:, 24:28]
        wix = small[:, 28:60]
        lb, oml = small[:, 60:64], small[:, 64:68]
        ghg = small[:, 68:72]
        sso, rso = small[:, 72:88], small[:, 88:104]
        nmx, esum = small[:, 104:136], small[:, 136:168]
        mx8 = small[:, 168:192]
        bst = small[:, 192:216]
        mhalf = small[:, 216:220]
        lbd = small[:, 220:224]
        resum = small[:, 224:226]
        ssy, rsy = small[:, 226:230], small[:, 230:234]
        ssf, rsf = small[:, 234:238], small[:, 238:242]

        ident = cst[:, K_IDENT:K_IDENT + P]
        reset = cst[:, K_RESET:K_RESET + T]
        causal = cst[:, K_CAUSAL:K_CAUSAL + P]
        flip = cst[:, K_FLIP:K_FLIP + P]

        bank = [ctx.enter_context(nc.psum_tensor(f"bank{b}", [P, 512], F32)) for b in range(8)]
        scratch = nc.dram_tensor("bias_rows", [AH, BT_LEN], F32).ap()

        raw_in = [sem(f"raw_in{s}") for s in range(SLOTS)]
        hi_done, lo_done, slab_used = sem("hi_done"), sem("lo_done"), sem("slab_used")
        full = [sem(f"full{b}") for b in range(8)]
        free = [sem(f"free{b}") for b in range(8)]
        const_in, fg_in, y_in, out_done = sem("const_in"), sem("fg_in"), sem("y_in"), sem("out_done")
        x_in = [sem(f"x_in{t}") for t in range(NT)]
        names = ("sq_done rs_done xn_done hTh_done cqn_done kd_done stat_done mv_done ikn_done wix_done "
                 "cqh_done acc_done causal_done max_done rep_done am_done lbd_done lbs_done lb_done ghg_done "
                 "f_done k_done ln_done scan_done th_done diff_done ex_done xm_done a_zero d0_done d1_done "
                 "e1_done qd_done kk_done ro_done on_done oah_done scr_done bt_in bm_done e_done "
                 "rsum_done obh_done mix_done mxh_done mxl_done hv_done hh_done hl_done fin_done rq_done "
                 "rik_done ry_done rf_done pool_step")
        S = {n: sem(n) for n in names.split()}
        SQ_X, SQ_CQ, SQ_HG, SQ_Y, SQ_F = 0, NT, 2 * NT, 2 * NT + 4 * HG, 3 * NT + 4 * HG

        side = {n: [] for n in range(NPLAN)}
        uses = [0] * 8

        def take(b):
            uses[b] += 1
            return b, uses[b] - 1

        tiles = {}
        for n, (kind, j) in enumerate(PLAN):
            if kind in ("c0", "hi", "hg") and j == 0 or kind == "wo" and j % 4 == 0:
                tiles[n] = [None] * NT
            elif kind in ("c0", "hi", "hg", "wo"):
                tiles[n] = n - 1 if isinstance(tiles[n - 1], list) else tiles[n - 1]
            elif kind == "c1":
                tiles[n] = "side"
            elif kind in ("hf", "hq", "ga", "gb"):
                tiles[n] = [None]
            elif kind in ("iq", "uq"):
                tiles[n] = [None] * 4
            else:
                tiles[n] = [None] * 2
        r = 0
        proj_use = [0] * 4
        for n in range(NPLAN):
            if isinstance(tiles[n], list):
                for q in range(len(tiles[n])):
                    b = r % 4
                    tiles[n][q] = (b, proj_use[b])
                    proj_use[b] += 1
                    r += 1
        for n in range(NPLAN):
            if isinstance(tiles[n], int):
                tiles[n] = tiles[tiles[n]]
        PRO = 1
        tiles = {n: v if v == "side" else [(b, u + PRO) for b, u in v] for n, v in tiles.items()}
        uses[4:8] = [PRO] * 4

        SIDEB = [4, 5, 6, 7]
        rot = [0]

        def nextb():
            b = SIDEB[rot[0] % 4]
            rot[0] += 1
            return take(b)

        n_c0, n_c1, n_hf, n_iq, n_uq = (AT_SLAB[k, 0] for k in ("c0", "c1", "hf", "iq", "uq"))
        n_hq, n_hi, n_hg, n_ga, n_ua, n_gb, n_ub, n_wo = (
            AT_SLAB[k, 0] for k in ("hq", "hi", "hg", "ga", "ua", "gb", "ub", "wo"))
        c1_bank = nextb()
        side[n_c1].append(("bias_rows", nextb(), nextb()))
        side[n_hf].append(("prep", ))
        side[n_hf + 1].append(("cqT", nextb(), nextb()))
        side[n_hf + 2].append(("kdT", nextb(), nextb(), nextb()))

        def spread(steps, first, last):
            span = last - first + 1
            for q, s in enumerate(steps):
                side[first + q * span // len(steps)].append(s)

        idx_units = [(i, h) for i in (1, 2, 3) for h in range(IH)]
        spread([("index", u, i, h, nextb()) for u, (i, h) in enumerate(idx_units)], n_uq, n_hi + 0)
        spread([("top", r_) for r_ in range(TOPK // 8)], n_hi + 1, n_ga + 3)
        spread([("log", j) for j in range(HG)], n_iq, n_iq)
        hgrn = []
        for l in range(LEVELS):
            hgrn.append(("diff", l))
            hgrn.append(("level", l, nextb(), nextb()))
        hgrn.append(("diag", [nextb() for _ in range(4)]))
        hgrn.append(("decays",))
        spread(hgrn, n_hi + 1, n_ga + 2)
        last_diag = hgrn[-2][1][-1]
        diag_banks = hgrn[-2][1]
        rec = [("chunk", c, nextb() if c < NT - 1 else None, nextb(), nextb() if c < NT - 1 else None)
               for c in range(NT)]
        spread(rec, n_ga + 3, n_ga + 6)
        side[n_ga + 7].append(("masks",))
        side[n_ga + 7].append(("oaT", [nextb() for _ in range(4)]))
        flips = [nextb() for _ in range(AH)]
        side[n_ua].append(("flip", flips))
        units = [(i, h) for i in range(NT) for h in range(AH)]
        NU = len(units)
        att = []
        for u in range(NU + 2):
            att.append(("attn", u,
                        take(4 + u % 2) if u < NU else None,
                        take(6) if 1 <= u <= NU else None,
                        take(7) if u >= 2 else None))
        spread(att, n_ua + 1, n_gb + 6)
        rot[0] = 0
        side[n_gb + 7].append(("obT", [nextb() for _ in range(4)]))
        mlp_bank = [(b, PRO + proj_use[b] if b < 4 else uses[b]) for b in range(8)]
        assert len({PRO + v for v in proj_use}) == 1
        MB = PRO + proj_use[0] + 1
        MB2 = [uses[4 + t] + 1 for t in range(NT)]

        by_count, seen = {}, 0
        for n, (kind, j) in enumerate(PLAN):
            if kind in ("c0", "hi", "hg", "wo") and j % 4 != 3:
                seen += 1
                by_count[n] = seen
        BY_COUNT = seen

        def used_up(n, it=None):
            if it is not None:
                m = n - NPLAN
                if m in (4, 6):
                    return slab_used, it * 2 + (BY_COUNT + m // 2 - 1)
                if m == 5:
                    return full[7], it + (MB2[3] + 1)
                if m in (-1, 7):
                    return full[3], it * 2 + (MB if m == -1 else MB + 2)
                return full[m], it * 2 + (MB + 1)
            if n in by_count:
                return slab_used, by_count[n]
            b, u = c1_bank if tiles[n] == "side" else tiles[n][-1]
            return full[b], u + 1

        def loop_blocks(eng, body):
            with eng.Fori(0, NFB - 1, 1) as it:
                body(it, False)
            body(NFB - 1, True)

        def W_of(i):
            return (i + 1) * P

        SC_OFF = [0, 128, 384, 768]

        def sc_of(i):
            return sc[:, SC_OFF[i]:SC_OFF[i] + W_of(i)]

        def heads_rows(h):
            return slice(64 * (h % 2), 64 * (h % 2) + 64)

        def slab_view(t, s, kt):
            return t[s][:, :].rearrange("p (k c) -> p k c", k=kt)

        hTh3 = hTh[:, :].rearrange("p (k t) -> p k t", k=KD_)
        hTl3 = hTl[:, :].rearrange("p (k t) -> p k t", k=KD_)
        cqh3 = cqh[:, :].rearrange("p (k t) -> p k t", k=2)
        cql3 = cql[:, :].rearrange("p (k t) -> p k t", k=2)
        oah3 = oah[:, :].rearrange("p (k t) -> p k t", k=HG)
        oal3 = oal[:, :].rearrange("p (k t) -> p k t", k=HG)
        obh3 = obh[:, :].rearrange("p (k t) -> p k t", k=4)
        obl3 = obl[:, :].rearrange("p (k t) -> p k t", k=4)
        mxh3 = mxh[:, :].rearrange("p (k t) -> p k t", k=KD_)
        mxl3 = mxl[:, :].rearrange("p (k t) -> p k t", k=KD_)
        hh3 = hh[:, :].rearrange("p (k t) -> p k t", k=4)
        hl3 = hl[:, :].rearrange("p (k t) -> p k t", k=4)
        c03 = c0s[:, :].rearrange("p (t c) -> p t c", t=NT)
        kd5 = kd[:, :].rearrange("p (t g u d) -> p t g u d", t=NT, g=GR, u=2)
        ikn4 = ikn[:, :].rearrange("p (t u d) -> p t u d", t=NT, u=2)
        iks3 = iks[:, :].rearrange("p (t c) -> p t c", t=NT)
        aq3 = aq[:, :].rearrange("p (j t) -> p j t", j=4)
        iq3 = iq[:, :].rearrange("p (j t) -> p j t", j=4)
        kdup3 = kdup[:, :].rearrange("p (g t) -> p g t", g=GR)
        y3 = y[:, :].rearrange("p (t c) -> p t c", t=NT)
        ys3 = ys[:, :].rearrange("p (t c) -> p t c", t=NT)
        xs3 = xs[:, :].rearrange("p (t c) -> p t c", t=NT)
        tha3 = tha[:, :].rearrange("p (m t) -> p m t", m=KD_)
        thb3 = thb[:, :].rearrange("p (m t) -> p m t", m=KD_)
        hV3 = hV[:, :].rearrange("p (t c) -> p t c", t=NT)
        hSG3 = hSG[:, :].rearrange("p (t c) -> p t c", t=NT)
        hO3 = hO[:, :].rearrange("p (t c) -> p t c", t=NT)
        ob3 = ob[:, :].rearrange("p (t c) -> p t c", t=NT)
        bt3 = bt[:, :].rearrange("p (h c) -> p h c", h=AH)
        hq_u = hQ[:, :].rearrange("p (u t) -> p u t", t=C)
        hk_u = hK[:, :].rearrange("p (u t) -> p u t", t=C)
        hf_u = hF[:, :].rearrange("p (u t) -> p u t", t=C)
        ha_u = hA[:, :].rearrange("p (u t) -> p u t", t=C)
        hx0_u = hX[0][:, :].rearrange("p (u t) -> p u t", t=C)
        x_t = x.rearrange("b (t p) d -> (b t) p d", p=P)
        out_t = out.rearrange("b (t p) d -> (b t) p d", p=P)

        block = ctx.enter_context(nc.Block())

        @block.sync
        def _(sp):
            sp.dma_start(cst[:, :], consts).then_inc(const_in, 16)
            for t in range(NT):
                sp.dma_start(xs3[:, t, :], x_t[t]).then_inc(x_in[t], 16)

            def load(n, dyn=None):
                s = n % SLOTS
                if n >= SLOTS:
                    sp.wait_ge(lo_done, n - SLOTS + 1 if dyn is None else dyn * PER_FB + (n - SLOTS + 1))
                sp.dma_start(raw[s][:, :], slabs[n] if dyn is None else
                             slabs[bass.ds(dyn * PER_FB + n, 1), :, :].rearrange("a p c -> (a p) c")
                             ).then_inc(raw_in[s], 16)

            for n in range(SLOTS):
                load(n)
            sp.dma_start(vec[:, :], vecs).then_inc(const_in, 16)
            sp.dma_start(oneh[:, :], onehot).then_inc(const_in, 16)
            sp.dma_start(rb[:, :], rel_bias).then_inc(const_in, 16)
            for n in range(SLOTS, NPLAN):
                load(n)
                if n == n_c1 + 4:
                    for b, u in side[n_c1][0][1:]:
                        sp.wait_ge(free[b], u + 1)
                    sp.dma_start(scratch, rbias[:, :]).then_inc(S["scr_done"], 16)
            sp.wait_ge(S["mxl_done"], KD_)
            sp.dma_start(fg[:, :], final_g.partition_broadcast(P)).then_inc(fg_in, 16)
            with sp.Fori(0, NFB, 1) as it:
                for m in range(PER_FB):
                    load(NPLAN + m, it)
            for t in range(NT):
                sp.wait_ge(S["fin_done"], t + 1)
                sp.dma_start(out_t[t], ys3[:, t, :]).then_inc(out_done, 16)
            sp.wait_ge(out_done, 16 * NT)

        @block.gpsimd
        def _(pool):
            pg = [0]

            def chain(ins):
                pg[0] += 1
                ins.then_inc(S["pool_step"], 1)
                pool.wait_ge(S["pool_step"], pg[0])

            def rsqrt_mean(dst, src, n, width):
                chain(pool.tensor_scalar(dst, src, 1.0 / width, EPS, ALU.mult, ALU.add))
                return pool.tensor_tensor(dst, dst, mhalf[:, 0:n], ALU.pow)

            chain(pool.memset(mhalf, -0.5))
            pool.memset(hA[:, :], 0.0).then_inc(S["a_zero"], 1)
            for t in range(NT):
                pool.wait_ge(S["sq_done"], SQ_X + t + 1)
                rsqrt_mean(rsx[:, t:t + 1], ssx[:, t:t + 1], 1, D).then_inc(S["rs_done"], 1)

            def do_side(s):
                if s[0] == "prep":
                    pool.wait_ge(S["sq_done"], SQ_CQ + NT)
                    rsqrt_mean(rsq, ssq, NT, QL).then_inc(S["rq_done"], 1)
                    for g in range(GR):
                        src = c03[:, :, QL + DH * g:QL + DH * g + DH].unsqueeze(2).to_broadcast([P, NT, 2, DH])
                        pool.tensor_copy(kd5[:, :, g], src).then_inc(S["kd_done"], 1)
                    pool.wait_ge(S["mv_done"], NT)
                    mv3 = mv.rearrange("p (t c) -> p t c", c=2)
                    rsqrt_mean(rik, mv3[:, :, 1], NT, 1).then_inc(S["rik_done"], 1)
                if s[0] == "index":
                    _, u, i, h, _ = s
                    if h == IH - 1:
                        pool.wait_ge(S["acc_done"], u + 1)
                        q = sc_of(i)[:, i * P:(i + 1) * P]
                        pool.affine_select(out=q, in_=q, compare_op=ALU.is_ge, fill=FILL, base=0,
                                           pattern=[[-1, P]], channel_multiplier=1).then_inc(S["causal_done"], 1)
                if s[0] == "chunk":
                    c = s[1]
                    pool.wait_ge(S["sq_done"], SQ_HG + HG * (c + 1))
                    rsqrt_mean(rso[:, 4 * c:4 * c + 4], sso[:, 4 * c:4 * c + 4], 4, P).then_inc(S["ro_done"], 1)
                if s[0] == "attn" and s[1] < NU:
                    u = s[1]
                    i, h = units[u]
                    if u == 0:
                        b, n_ = flips[-1]
                        pool.wait_ge(free[b], n_ + 1)
                        pool.wait_ge(S["am_done"], 4)
                        b, n_ = rec[NT - 1][3]
                        pool.wait_ge(full[b], n_ + 1)
                    if u >= 2:
                        b, n_ = att[u - 2][2]
                        pool.wait_ge(free[b], n_ + 1)
                    pool.tensor_tensor(bm[u % 2][:, 0:W_of(i)], bt3[:, h, T - W_of(i):T], sc_of(i),
                                       ALU.add).then_inc(S["bm_done"], 1)

            for n in range(NPLAN):
                for s in side[n]:
                    do_side(s)
            pool.wait_ge(S["sq_done"], SQ_Y + NT)
            rsqrt_mean(rsy, ssy, NT, D).then_inc(S["ry_done"], 1)
            pool.wait_ge(S["sq_done"], SQ_F + NT)
            rsqrt_mean(rsf, ssf, NT, D).then_inc(S["rf_done"], 1)

        @block.scalar
        def _(act):
            def hi(n, it=None):
                s = n % SLOTS
                arrived = 16 * (n // SLOTS + 1)
                act.wait_ge(raw_in[s], arrived if it is None else it * (16 * PER_FB // SLOTS) + arrived)
                if n >= SLOTS:
                    act.wait_ge(*used_up(n - SLOTS, it))
                act.copy(whi[s][:, :], raw[s][:, :]).then_inc(hi_done, 1)

            def wait_full(bu):
                act.wait_ge(full[bu[0]], bu[1] + 1)

            squares = [0]

            def square(src, width, acc):
                if squares[0]:
                    act.wait_ge(S["sq_done"], squares[0])
                squares[0] += 1
                act.activation(junk[:, 0:width], src, ACT.Square, accum_out=acc).then_inc(S["sq_done"], 1)

            for t in range(NT):
                act.wait_ge(x_in[t], 16)
                square(xs3[:, t, :], D, ssx[:, t:t + 1])
            for n in range(AHEAD):
                hi(n)
            act.wait_ge(const_in, 64)
            for k in range(KD_):
                act.wait_ge(full[k], 1)
                act.activation(hTh3[:, k, :], bank[k][:, :], ACT.Copy,
                               scale=vec[:, V_ATTN + k:V_ATTN + k + 1]).then_inc(S["hTh_done"], 1)

            def copy_out(dst, bu, signal, **kw):
                wait_full(bu)
                act.activation(dst, bank[bu[0]][:, :], kw.pop("func", ACT.Copy), **kw).then_inc(S[signal], 1)

            def evict(n):
                kind, j = PLAN[n]
                if kind == "c0" and j == 3:
                    for t in range(NT):
                        b, u = tiles[n][t]
                        wait_full((b, u))
                        act.activation(c03[:, t, :], bank[b][:, :], ACT.Copy).then_inc(free[b], 1)
                    for t in range(NT):
                        b, u = tiles[n][t]
                        act.wait_ge(free[b], u + 1)
                        square(c03[:, t, 0:QL], QL, ssq[:, t:t + 1])
                if kind == "c1":
                    b, u = c1_bank
                    wait_full(c1_bank)
                    act.activation(iks[:, :], bank[b][:, 0:NT * 72], ACT.Copy).then_inc(free[b], 1)
                    act.wait_ge(S["lbd_done"], 1)
                    act.activation(lb, lbd, ACT.Sigmoid).then_inc(S["lbs_done"], 1)
                if kind == "hf":
                    b, u = tiles[n][0]
                    wait_full((b, u))
                    act.activation(hF[:, j * T:(j + 1) * T], bank[b][:, :], ACT.Sigmoid).then_inc(free[b], 1)
                if kind == "iq":
                    for q, (b, u) in enumerate(tiles[n]):
                        wait_full((b, u))
                        act.activation(iq3[:, q, :], bank[b][:, :], ACT.Copy).then_inc(free[b], 1)
                if kind == "hq":
                    b, u = tiles[n][0]
                    wait_full((b, u))
                    act.activation(hQ[:, j * T:(j + 1) * T], bank[b][:, :], ACT.Copy).then_inc(free[b], 1)
                if kind == "hi" and j == 3:
                    for t, (b, u) in enumerate(tiles[n]):
                        wait_full((b, u))
                        act.activation(hV3[:, t, :], bank[b][:, :], ACT.Copy).then_inc(free[b], 1)
                if kind == "hg" and j == 3:
                    for t, (b, u) in enumerate(tiles[n]):
                        wait_full((b, u))
                        act.activation(hSG3[:, t, :], bank[b][:, :], ACT.Tanh, scale=0.5).then_inc(S["th_done"], 1)
                if kind == "ga":
                    b, u = tiles[n][0]
                    wait_full((b, u))
                    if j == 0:
                        act.wait_ge(S["acc_done"], len(idx_units))
                        act.wait_ge(S["scr_done"], 16)
                    act.activation(tha3[:, j, :], bank[b][:, :], ACT.Tanh, scale=0.5).then_inc(free[b], 1)
                if kind == "gb":
                    b, u = tiles[n][0]
                    wait_full((b, u))
                    act.activation(thb3[:, j, :], bank[b][:, :], ACT.Tanh, scale=0.5).then_inc(free[b], 1)
                if kind == "ub":
                    for q, (b, u) in enumerate(tiles[n]):
                        m = 2 * j + q
                        act.wait_ge(S["mix_done"], m + 1)
                        act.activation(mxh3[:, m, :], tha3[:, m, :], ACT.Copy).then_inc(S["mxh_done"], 1)
                    if j == 3:
                        act.dma_start(y3[:, :, :], x.rearrange("b (t p) d -> p (b t) d", p=P)).then_inc(y_in, 16)

            def do_side(s):
                k = s[0]
                if k == "cqT":
                    for q in range(2):
                        copy_out(cqh3[:, q, :], s[1 + q], "cqh_done", scale=vec[:, V_Q + q:V_Q + q + 1])
                if k == "kdT":
                    for g in range(GR):
                        b, u = s[1 + g]
                        wait_full(s[1 + g])
                        act.activation(kdup3[:, g, :], bank[b][:, :], ACT.Copy).then_inc(free[b], 1)
                if k == "index":
                    _, u, i, h, (b, n_) = s
                    wait_full((b, n_))
                    if u >= 2:
                        act.wait_ge(S["acc_done"], u - 1)
                    act.activation(rel[u % 2][:, 0:W_of(i)], bank[b][:, 0:W_of(i)], ACT.Relu,
                                   scale=DH ** -0.5).then_inc(free[b], 1)
                if k == "log":
                    j = s[1]
                    act.wait_ge(S["k_done"], j + 1)
                    f = hF[:, j * T:(j + 1) * T]
                    act.activation(f, f, ACT.Ln).then_inc(S["ln_done"], 1)
                if k == "diff":
                    l = s[1]
                    act.wait_ge(S["diff_done"], 2 * (l + 1))
                    act.activation(hX[l % 2][:, :], hX[l % 2][:, :], ACT.Exp).then_inc(S["ex_done"], 1)
                if k == "decays":
                    wait_full(last_diag)
                    act.activation(hX[0][:, :], hF[:, :], ACT.Exp).then_inc(S["d0_done"], 1)
                    act.wait_ge(S["d1_done"], 1)
                    act.activation(hX[1][:, :], hX[1][:, :], ACT.Exp).then_inc(S["e1_done"], 1)
                if k == "chunk":
                    _, c, bk, bo, bs = s
                    if c < NT - 1:
                        wait_full(bk)
                        if c:
                            wait_full(rec[c - 1][4])
                        act.activation(hKT[:, :], bank[bk[0]][:, :], ACT.Copy).then_inc(free[bk[0]], 1)
                    wait_full(bo)
                    if c == 0:
                        act.wait_ge(S["d0_done"], 1)
                        act.wait_ge(S["d1_done"], 1)
                    act.activation(hO3[:, c, :], bank[bo[0]][:, :], ACT.Copy).then_inc(free[bo[0]], 1)
                    act.wait_ge(free[bo[0]], bo[1] + 1)
                    for h in range(HG):
                        q = HG * c + h
                        square(hO3[:, c, h * P:(h + 1) * P], P, sso[:, q:q + 1])
                if k == "oaT":
                    b, u = rec[NT - 2][4]
                    act.wait_ge(free[b], u + 1)
                    act.wait_ge(S["ghg_done"], 1)
                    act.wait_ge(S["scr_done"], 16)
                    src = bass.AP(tensor=scratch.tensor, offset=0, ap=[[1, P], [BT_LEN, AH], [1, T]])
                    act.dma_start(bt3[:, :, :], src).then_inc(S["bt_in"], 16)
                    for h in range(HG):
                        copy_out(oah3[:, h, :], s[1][h], "oah_done", scale=ghg[:, h:h + 1])
                if k == "flip":
                    for h in range(AH):
                        b, u = flips[h]
                        wait_full((b, u))
                        act.activation(bt3[:, h, :], bank[b][:, :], ACT.Copy).then_inc(free[b], 1)
                if k == "attn":
                    _, u, bq, btp, bv = s
                    if u < NU:
                        i, h = units[u]
                        act.wait_ge(free[bq[0]], bq[1] + 1)
                        w = W_of(i)
                        act.activation(tt[u % 2][:, 0:w], tt[u % 2][:, 0:w], ACT.Exp, scale=-1.0,
                                       bias=nmx[:, u:u + 1], accum_out=esum[:, u:u + 1]).then_inc(S["e_done"], 1)
                    if btp is not None:
                        v = u - 1
                        i, h = units[v]
                        wait_full(btp)
                        if v >= 2:
                            wait_full(att[v][4])
                        act.activation(et[v % 2][:, 0:W_of(i)], bank[6][:, 0:W_of(i)],
                                       ACT.Copy).then_inc(free[6], 1)
                if k == "obT":
                    for q in range(4):
                        copy_out(obh3[:, q, :], s[1][q], "obh_done")

            for n in range(NPLAN):
                hi(n + AHEAD)
                for s in side[n]:
                    do_side(s)
                evict(n)
            for t in range(NT):
                b, u = tiles[n_wo + 7][t]
                act.wait_ge(free[b], u + 1)
                square(y3[:, t, :], D, ssy[:, t:t + 1])
            for k in range(KD_):
                copy_out(hTh3[:, k, :], mlp_bank[k], "hTh_done", scale=vec[:, V_MLP + k:V_MLP + k + 1])

            def block_(it, last):
                for m in range(PER_FB):
                    if not (last and m + AHEAD >= PER_FB):
                        hi(NPLAN + m + AHEAD, it)
                    if m < 4:
                        act.wait_ge(full[m], it * 2 + (MB + 1))
                        act.activation(rt[m % 2][:, :], bank[m][:, :], ACT.Relu).then_inc(free[m], 1)
                        act.wait_ge(S["hv_done"], it * 4 + (m + 1))
                        act.activation(hh3[:, m, :], hv[m % 2][:, :], ACT.Copy).then_inc(S["hh_done"], 1)

            loop_blocks(act, block_)
            for t in range(NT):
                act.wait_ge(free[t], MB + 2 * NFB)
                square(y3[:, t, :], D, ssf[:, t:t + 1])

        @block.vector
        def _(dve):
            def lo(n, it=None):
                s = n % SLOTS
                dve.wait_ge(hi_done, n + 1 if it is None else it * PER_FB + (n + 1))
                dve.tensor_tensor(wlo[s][:, :], raw[s][:, :], whi[s][:, :].bitcast(F32),
                                  ALU.subtract).then_inc(lo_done, 1)

            def wait_full(bu):
                dve.wait_ge(full[bu[0]], bu[1] + 1)

            dve.wait_ge(const_in, 64)
            dve.tensor_tensor(lbd, vec[:, V_LB0:V_LB0 + 4], vec[:, V_LB1:V_LB1 + 4],
                              ALU.subtract).then_inc(S["lbd_done"], 1)
            dve.tensor_scalar(ghg, vec[:, V_HG:V_HG + 4], 0.5, None, ALU.mult).then_inc(S["ghg_done"], 1)
            for t in range(NT):
                dve.wait_ge(S["rs_done"], t + 1)
                dve.tensor_scalar(xs3[:, t, :], xs3[:, t, :], rsx[:, t:t + 1], None,
                                  ALU.mult).then_inc(S["xn_done"], 1)
            for n in range(AHEAD):
                lo(n)

            def lo_scaled(dst, bu, scale, hi_ap, hi_sem, val):
                dve.wait_ge(S[hi_sem], val)
                dve.scalar_tensor_tensor(out=dst, in0=bank[bu[0]][:, :], scalar=scale, in1=hi_ap.bitcast(F32),
                                         op0=ALU.mult, op1=ALU.subtract).then_inc(free[bu[0]], 1)

            for k in range(KD_):
                lo_scaled(hTl3[:, k, :], (k, 0), vec[:, V_ATTN + k:V_ATTN + k + 1], hTh3[:, k, :], "hTh_done", k + 1)

            def evict(n):
                kind, j = PLAN[n]
                if kind == "c1":
                    dve.wait_ge(S["lbs_done"], 1)
                    dve.tensor_scalar(oml, lb, -1.0, 1.0, ALU.mult, ALU.add).then_inc(S["lb_done"], 1)
                if kind == "hf":
                    b, u = tiles[n][0]
                    f, k = hF[:, j * T:(j + 1) * T], hK[:, j * T:(j + 1) * T]
                    dve.wait_ge(free[b], u + 1)
                    dve.wait_ge(S["lb_done"], 1)
                    dve.tensor_scalar(f, f, oml[:, j:j + 1], lb[:, j:j + 1], ALU.mult, ALU.add).then_inc(S["f_done"], 1)
                    dve.wait_ge(S["f_done"], j + 1)
                    dve.tensor_scalar(k, f, -1.0, 1.0, ALU.mult, ALU.add).then_inc(S["k_done"], 1)
                if kind == "uq":
                    for q, (b, u) in enumerate(tiles[n]):
                        wait_full((b, u))
                        dve.tensor_scalar(aq3[:, q, :], bank[b][:, :], DH ** -0.5, None, ALU.mult).then_inc(free[b], 1)
                if kind == "hg" and j == 3:
                    for t, (b, u) in enumerate(tiles[n]):
                        dve.wait_ge(S["th_done"], t + 1)
                        dve.scalar_tensor_tensor(out=hSG3[:, t, :], in0=hSG3[:, t, :], scalar=1.0, in1=bank[b][:, :],
                                                 op0=ALU.add, op1=ALU.mult).then_inc(free[b], 1)
                if kind == "ua":
                    for q, (b, u) in enumerate(tiles[n]):
                        m = 2 * j + q
                        wait_full((b, u))
                        gb, gu = tiles[n_ga + m][0]
                        dve.wait_ge(free[gb], gu + 1)
                        dve.scalar_tensor_tensor(out=tha3[:, m, :], in0=tha3[:, m, :], scalar=1.0, in1=bank[b][:, :],
                                                 op0=ALU.add, op1=ALU.mult).then_inc(free[b], 1)
                if kind == "ub":
                    for q, (b, u) in enumerate(tiles[n]):
                        m = 2 * j + q
                        wait_full((b, u))
                        gb, gu = tiles[n_gb + m][0]
                        dve.wait_ge(free[gb], gu + 1)
                        dve.scalar_tensor_tensor(out=thb3[:, m, :], in0=thb3[:, m, :], scalar=1.0, in1=bank[b][:, :],
                                                 op0=ALU.add, op1=ALU.mult).then_inc(free[b], 1)
                        dve.wait_ge(free[b], u + 1)
                        dve.tensor_tensor(tha3[:, m, :], tha3[:, m, :], thb3[:, m, :], ALU.add).then_inc(S["mix_done"], 1)
                        dve.wait_ge(S["mxh_done"], m + 1)
                        dve.tensor_tensor(mxl3[:, m, :], tha3[:, m, :], mxh3[:, m, :].bitcast(F32),
                                          ALU.subtract).then_inc(S["mxl_done"], 1)
                if kind == "wo" and j % 4 == 3:
                    half = j // 4
                    if half == 0:
                        dve.wait_ge(y_in, 16)
                    for t, (b, u) in enumerate(tiles[n]):
                        wait_full((b, u))
                        yy = y3[:, t, half * 512:(half + 1) * 512]
                        dve.scalar_tensor_tensor(out=yy, in0=bank[b][:, :], scalar=0.5, in1=yy,
                                                 op0=ALU.mult, op1=ALU.add).then_inc(free[b], 1)

            def do_side(s):
                k = s[0]
                if k == "bias_rows":
                    for q, (w0, w1) in enumerate(((0, 512), (512, BT_LEN))):
                        b, u = s[1 + q]
                        wait_full(s[1 + q])
                        dve.tensor_copy(rbias[:, w0:w1], bank[b][0:AH, 0:w1 - w0]).then_inc(free[b], 1)
                if k == "prep":
                    dve.wait_ge(S["rq_done"], 1)
                    for t in range(NT):
                        q = c03[:, t, 0:QL]
                        dve.tensor_scalar(q, q, rsq[:, t:t + 1], None, ALU.mult).then_inc(S["cqn_done"], 1)
                    b, u = c1_bank
                    dve.wait_ge(free[b], u + 1)
                    dve.tensor_scalar(wix.rearrange("p (t h) -> p t h", t=NT), iks3[:, :, DH:DH + IH],
                                      IH ** -0.5, None, ALU.mult).then_inc(S["wix_done"], 1)
                    for t in range(NT):
                        dve.bn_stats(bst[:, 6 * t:6 * t + 6], iks3[:, t, 0:DH]).then_inc(S["stat_done"], 1)
                    for t in range(NT):
                        dve.wait_ge(S["stat_done"], t + 1)
                        dve.bn_aggr(mv[:, 2 * t:2 * t + 2], bst[:, 6 * t:6 * t + 6]).then_inc(S["mv_done"], 1)
                    dve.wait_ge(S["rik_done"], 1)
                    for t in range(NT):
                        dve.tensor_scalar(ikn4[:, t], iks3[:, t, 0:DH].unsqueeze(1).to_broadcast([P, 2, DH]),
                                          mv[:, 2 * t:2 * t + 1], rik[:, t:t + 1], ALU.subtract,
                                          ALU.mult).then_inc(S["ikn_done"], 1)
                if k == "cqT":
                    for q in range(2):
                        lo_scaled(cql3[:, q, :], s[1 + q], vec[:, V_Q + q:V_Q + q + 1], cqh3[:, q, :], "cqh_done", q + 1)
                if k == "kdT":
                    b, u = s[3]
                    wait_full(s[3])
                    dve.tensor_scalar(ikd[:, :], bank[b][:, :], vec[:, V_IKG:V_IKG + 1], vec[:, V_IKB:V_IKB + 1],
                                      ALU.mult, ALU.add).then_inc(free[b], 1)
                if k == "index":
                    _, u, i, h, (b, n_) = s
                    dve.wait_ge(free[b], n_ + 1)
                    w = wix[:, i * IH + h:i * IH + h + 1]
                    r_ = rel[u % 2][:, 0:W_of(i)]
                    if h == 0:
                        dve.tensor_scalar(sc_of(i), r_, w, None, ALU.mult).then_inc(S["acc_done"], 1)
                    else:
                        dve.wait_ge(S["acc_done"], u)
                        dve.scalar_tensor_tensor(out=sc_of(i), in0=r_, scalar=w, in1=sc_of(i), op0=ALU.mult,
                                                 op1=ALU.add).then_inc(S["acc_done"], 1)
                if k == "top":
                    r_ = s[1]
                    for i in (1, 2, 3):
                        q = 3 * r_ + i - 1
                        if r_ == 0:
                            dve.wait_ge(S["causal_done"], i)
                        else:
                            dve.wait_ge(S["rep_done"], q - 2)
                        dve.max(mx8[:, 8 * (i - 1):8 * i], sc_of(i)).then_inc(S["max_done"], 1)
                    for i in (1, 2, 3):
                        q = 3 * r_ + i - 1
                        dve.wait_ge(S["max_done"], q + 1)
                        dve.match_replace(sc_of(i), mx8[:, 8 * (i - 1):8 * i], sc_of(i), TAKEN).then_inc(S["rep_done"], 1)
                if k == "masks":
                    dve.tensor_copy(sc_of(0), causal).then_inc(S["am_done"], 1)
                    dve.wait_ge(S["rep_done"], 3 * (TOPK // 8))
                    for i in (1, 2, 3):
                        dve.tensor_scalar(sc_of(i), sc_of(i), (FILL + TAKEN) / 2, NEG, ALU.is_gt,
                                          ALU.mult).then_inc(S["am_done"], 1)
                if k == "log":
                    j = s[1]
                    dve.wait_ge(S["ln_done"], j + 1)
                    f = hF[:, j * T:(j + 1) * T]
                    dve.tensor_tensor_scan(f, reset, f, 0.0, ALU.mult, ALU.add).then_inc(S["scan_done"], 1)
                if k == "diff":
                    l = s[1]
                    B, H = 2 << l, 1 << l
                    dve.wait_ge(S["scan_done"], HG)
                    if l >= 2:
                        wait_full(hgrn[2 * (l - 2) + 1][3])
                    f = hF[:, :].rearrange("p (n b) -> p n b", b=B)
                    xx = hX[l % 2][:, :].rearrange("p (n b) -> p n b", b=B)
                    mid = f[:, :, H - 1:H].to_broadcast([P, HG * T // B, H])
                    dve.tensor_tensor(xx[:, :, H:B], f[:, :, H:B], mid, ALU.subtract).then_inc(S["diff_done"], 1)
                    dve.tensor_tensor(xx[:, :, 0:H], mid, f[:, :, 0:H], ALU.subtract).then_inc(S["diff_done"], 1)
                if k == "level":
                    _, l, b0, b1 = s
                    B, H = 2 << l, 1 << l
                    xx = hX[l % 2][:, :].rearrange("p (n b) -> p n b", b=B)
                    q3 = hQ[:, :].rearrange("p (n b) -> p n b", b=B)
                    k3 = hK[:, :].rearrange("p (n b) -> p n b", b=B)
                    dve.wait_ge(S["ex_done"], l + 1)
                    if l == 0:
                        for q_ in range(4):
                            b_, u_ = tiles[n_hq + q_][0]
                            dve.wait_ge(free[b_], u_ + 1)
                    dve.tensor_tensor(xx[:, :, H:B], xx[:, :, H:B], q3[:, :, H:B], ALU.mult).then_inc(S["xm_done"], 1)
                    dve.tensor_tensor(xx[:, :, 0:H], xx[:, :, 0:H], k3[:, :, 0:H], ALU.mult).then_inc(S["xm_done"], 1)
                    if l == 0:
                        dve.wait_ge(S["a_zero"], 1)
                    mask = cst[:, K_MASK + 64 * l:K_MASK + 64 * l + 64].rearrange("p (n h) -> p n h", h=H)
                    mask = mask.unsqueeze(1).to_broadcast([P, 8, C // B, H]).bitcast(I32)
                    for q, bu in enumerate((b0, b1)):
                        wait_full(bu)
                        dst = ha_u[:, 8 * q:8 * q + 8, :].rearrange("p u (n b) -> p u n b", b=B)[:, :, :, H:B]
                        src = bank[bu[0]][:, :].rearrange("p (u n h) -> p u n h", u=8, h=H)
                        dve.copy_predicated(dst, mask, src).then_inc(free[bu[0]], 1)
                if k == "diag":
                    mask = ident.unsqueeze(1).to_broadcast([P, 4, C]).bitcast(I32)
                    b, u = hgrn[-3][3]
                    dve.wait_ge(free[b], u + 1)
                    for q, bu in enumerate(s[1]):
                        wait_full(bu)
                        dve.copy_predicated(ha_u[:, 4 * q:4 * q + 4, :], mask,
                                            bank[bu[0]][:, :].rearrange("p (u t) -> p u t", u=4)).then_inc(free[bu[0]], 1)
                if k == "decays":
                    wait_full(last_diag)
                    dve.tensor_tensor(hX[1][:, :].rearrange("p (u t) -> p u t", t=C),
                                      hf_u[:, :, C - 1:C].to_broadcast([P, 16, C]), hf_u[:, :, :],
                                      ALU.subtract).then_inc(S["d1_done"], 1)
                    dve.wait_ge(S["d0_done"], 1)
                    dve.tensor_tensor(hQ[:, :], hQ[:, :], hX[0][:, :], ALU.mult).then_inc(S["qd_done"], 1)
                    dve.wait_ge(S["e1_done"], 1)
                    dve.tensor_tensor(hK[:, :], hK[:, :], hX[1][:, :], ALU.mult).then_inc(S["kk_done"], 1)
                if k == "chunk":
                    _, c, bk, bo, bs = s
                    if c < NT - 1:
                        wait_full(bs)
                        for h in range(HG):
                            st = hS[:, h * P:(h + 1) * P]
                            ps = bank[bs[0]][:, h * P:(h + 1) * P]
                            if c == 0:
                                ins = dve.tensor_copy(st, ps)
                            else:
                                dve.wait_ge(full[bo[0]], bo[1] + 1)
                                dec = hx0_u[:, h * NT + c, C - 1:C]
                                ins = dve.scalar_tensor_tensor(out=st, in0=st, scalar=dec, in1=ps, op0=ALU.mult,
                                                               op1=ALU.add)
                        ins.then_inc(free[bs[0]], 1)
                    dve.wait_ge(S["ro_done"], c + 1)
                    for h in range(HG):
                        o = hO3[:, c, h * P:(h + 1) * P]
                        dve.scalar_tensor_tensor(out=o, in0=o, scalar=rso[:, 4 * c + h:4 * c + h + 1],
                                                 in1=hSG3[:, c, h * P:(h + 1) * P], op0=ALU.mult,
                                                 op1=ALU.mult).then_inc(S["on_done"], 1)
                if k == "oaT":
                    for h in range(HG):
                        lo_scaled(oal3[:, h, :], s[1][h], ghg[:, h:h + 1], oah3[:, h, :], "oah_done", h + 1)
                if k == "attn":
                    _, u, bq, btp, bv = s
                    if u < NU:
                        i, h = units[u]
                        w = W_of(i)
                        wait_full(bq)
                        dve.wait_ge(S["bm_done"], u + 1)
                        if u >= 2:
                            wait_full(att[u - 1][3])
                        dve.tensor_tensor_reduce(tt[u % 2][:, 0:w], bank[bq[0]][:, 0:w], bm[u % 2][:, 0:w], -1.0,
                                                 3.4e38, ALU.add, ALU.min, nmx[:, u:u + 1]).then_inc(free[bq[0]], 1)
                    if bv is not None:
                        v = u - 2
                        i, h = units[v]
                        dve.wait_ge(S["e_done"], v + 1)
                        if v >= 2:
                            dve.wait_ge(free[7], att[v][4][1] + 1)
                        dve.reciprocal(resum[:, v % 2:v % 2 + 1], esum[:, v:v + 1]).then_inc(S["rsum_done"], 1)
                        wait_full(bv)
                        dve.wait_ge(S["rsum_done"], v + 1)
                        dve.tensor_scalar(ob3[:, i, h * DH:(h + 1) * DH], bank[7][:, 0:DH], resum[:, v % 2:v % 2 + 1],
                                          None, ALU.mult).then_inc(free[7], 1)
                if k == "obT":
                    for q in range(4):
                        b, u = s[1][q]
                        dve.wait_ge(S["obh_done"], q + 1)
                        dve.tensor_tensor(obl3[:, q, :], bank[b][:, :], obh3[:, q, :].bitcast(F32),
                                          ALU.subtract).then_inc(free[b], 1)

            for n in range(NPLAN):
                lo(n + AHEAD)
                for s in side[n]:
                    do_side(s)
                evict(n)
            dve.wait_ge(S["ry_done"], 1)
            for t in range(NT):
                dve.tensor_scalar(ys3[:, t, :], y3[:, t, :], rsy[:, t:t + 1], None, ALU.mult).then_inc(S["xn_done"], 1)
            for k in range(KD_):
                lo_scaled(hTl3[:, k, :], mlp_bank[k], vec[:, V_MLP + k:V_MLP + k + 1], hTh3[:, k, :], "hTh_done",
                          KD_ + k + 1)

            def block_(it, last):
                for m in range(PER_FB):
                    if not (last and m + AHEAD >= PER_FB):
                        lo(NPLAN + m + AHEAD, it)
                    if m < 4:
                        dve.wait_ge(free[m], it * 2 + (MB + 1))
                        if m:
                            dve.wait_ge(S["hl_done"], it * 4 + m)
                        dve.tensor_tensor(hv[m % 2][:, :], rt[m % 2][:, :], rt[m % 2][:, :],
                                          ALU.mult).then_inc(S["hv_done"], 1)
                        dve.wait_ge(S["hh_done"], it * 4 + (m + 1))
                        dve.tensor_tensor(hl3[:, m, :], hv[m % 2][:, :], hh3[:, m, :].bitcast(F32),
                                          ALU.subtract).then_inc(S["hl_done"], 1)
                    if m in (5, 7):
                        half = (m - 5) // 2
                        if half == 0:
                            dve.wait_ge(S["hl_done"], it * 4 + 4)
                        for t in range(NT):
                            if half == 0:
                                b = 4 + t
                                dve.wait_ge(full[b], it + (MB2[t] + 1))
                            else:
                                b = t
                                dve.wait_ge(full[b], it * 2 + (MB + 2))
                            yy = y3[:, t, half * 512:(half + 1) * 512]
                            dve.tensor_tensor(yy, yy, bank[b][:, :], ALU.add).then_inc(free[b], 1)

            loop_blocks(dve, block_)
            dve.wait_ge(S["rf_done"], 1)
            dve.wait_ge(fg_in, 16)
            for t in range(NT):
                dve.scalar_tensor_tensor(out=ys3[:, t, :], in0=y3[:, t, :], scalar=rsf[:, t:t + 1], in1=fg[:, :],
                                         op0=ALU.mult, op1=ALU.mult).then_inc(S["fin_done"], 1)

        @block.tensor
        def _(pe):
            def wait_free(bu):
                if bu[1]:
                    pe.wait_ge(free[bu[0]], bu[1])

            def three(dst, lh, ll, rh, rl, start, stop):
                pe.matmul(dst, lh, rh, start=start, stop=False)
                pe.matmul(dst, lh, rl, start=False, stop=False)
                return pe.matmul(dst, ll, rh, start=False, stop=stop)

            def transposes(dst_bu, srcs):
                wait_free(dst_bu)
                for q, src in enumerate(srcs):
                    last = pe.transpose(bank[dst_bu[0]][:, q * P:(q + 1) * P], src, ident)
                last.then_inc(full[dst_bu[0]], 1)

            pe.wait_ge(const_in, 64)
            pe.wait_ge(S["xn_done"], NT)
            for k in range(KD_):
                transposes((k, 0), [xs3[:, t, k * P:(k + 1) * P] for t in range(NT)])

            def token_slab(n, hi_, lo_, ts, k0, first, last):
                s = n % SLOTS
                wh, wl = slab_view(whi, s, 2), slab_view(wlo, s, 2)
                order = [(kk, t) for kk in range(2) for t in range(NT)]
                for kk, t in order:
                    b, u = ts[t]
                    st, sp_ = first and kk == 0, last and kk == 1
                    if st:
                        wait_free((b, u))
                    k = k0 + kk
                    ins = three(bank[b][:, :], hi_[:, k, t * P:(t + 1) * P], lo_[:, k, t * P:(t + 1) * P],
                                wh[:, kk, :], wl[:, kk, :], st, sp_)
                    if sp_:
                        ins.then_inc(full[b], 1)
                return ins

            def feature_tile(bu, hi_, lo_, wh, wl, kt, c0):
                b = bu[0]
                wait_free(bu)
                for k in range(kt):
                    ins = three(bank[b][:, :], wh[:, k, c0:c0 + P], wl[:, k, c0:c0 + P], hi_[:, k, :], lo_[:, k, :],
                                k == 0, k == kt - 1)
                return ins.then_inc(full[b], 1)

            def mms(n):
                kind, j = PLAN[n]
                s = n % SLOTS
                pe.wait_ge(lo_done, n + 1)
                if n == 0:
                    for b in range(8):
                        pe.wait_ge(free[b], 1)
                if kind in ("c0", "hi", "hg"):
                    ins = token_slab(n, hTh3, hTl3, tiles[n], 2 * j, j == 0, j == 3)
                elif kind == "c1":
                    b, u = c1_bank
                    wait_free(c1_bank)
                    wh = whi[s][:, 0:KD_ * 72].rearrange("p (k c) -> p k c", k=KD_)
                    wl = wlo[s][:, 0:KD_ * 72].rearrange("p (k c) -> p k c", k=KD_)
                    for t in range(NT):
                        for k in range(KD_):
                            ins = three(bank[b][:, t * 72:(t + 1) * 72], hTh3[:, k, t * P:(t + 1) * P],
                                        hTl3[:, k, t * P:(t + 1) * P], wh[:, k, :], wl[:, k, :], k == 0, k == KD_ - 1)
                    ins.then_inc(full[b], 1)
                elif kind in ("hf", "hq", "ga", "gb"):
                    ins = feature_tile(tiles[n][0], hTh3, hTl3, slab_view(whi, s, KD_), slab_view(wlo, s, KD_), KD_, 0)
                elif kind in ("iq", "uq"):
                    if kind == "iq":
                        bq = [x_ for x_ in side[n_hf + 1] if x_[0] == "cqT"][0]
                        for q in (1, 2):
                            pe.wait_ge(free[bq[q][0]], bq[q][1] + 1)
                    for q in range(4):
                        ins = feature_tile(tiles[n][q], cqh3, cql3, slab_view(whi, s, 2), slab_view(wlo, s, 2), 2, q * P)
                elif kind in ("ua", "ub"):
                    h_, l_ = (oah3, oal3) if kind == "ua" else (obh3, obl3)
                    if j == 0:
                        step = [x_ for x_ in side[n - 1] if x_[0] == ("oaT" if kind == "ua" else "obT")][0]
                        for b, u in step[1]:
                            pe.wait_ge(free[b], u + 1)
                    for q in range(2):
                        ins = feature_tile(tiles[n][q], h_, l_, slab_view(whi, s, 4), slab_view(wlo, s, 4), 4, q * P)
                elif kind == "wo":
                    if j < 4:
                        pe.wait_ge(S["mxl_done"], 2 * j + 2)
                    ins = token_slab(n, mxh3, mxl3, tiles[n], 2 * (j % 4), j % 4 == 0, j % 4 == 3)
                if n in by_count:
                    ins.then_inc(slab_used, 1)

            def do_side(s):
                k = s[0]
                if k == "bias_rows":
                    for q, (w0, w1) in enumerate(((0, 512), (512, BT_LEN))):
                        b, u = s[1 + q]
                        wait_free(s[1 + q])
                        pe.matmul(bank[b][0:AH, 0:w1 - w0], rb[:, :], oneh[:, w0:w1], start=True,
                                  stop=True).then_inc(full[b], 1)
                if k == "cqT":
                    pe.wait_ge(S["cqn_done"], NT)
                    for q in range(2):
                        transposes(s[1 + q], [c03[:, t, q * P:(q + 1) * P] for t in range(NT)])
                if k == "kdT":
                    pe.wait_ge(S["kd_done"], GR)
                    for g in range(GR):
                        transposes(s[1 + g], [kd5[:, t, g].rearrange("p u d -> p (u d)") for t in range(NT)])
                    pe.wait_ge(S["ikn_done"], NT)
                    transposes(s[3], [ikn4[:, t].rearrange("p u d -> p (u d)") for t in range(NT)])
                if k == "index":
                    _, u, i, h, (b, n_) = s
                    if u == 0:
                        for q in range(4):
                            b_, u_ = tiles[n_iq][q]
                            pe.wait_ge(free[b_], u_ + 1)
                        b_, u_ = [x_ for x_ in side[n_hf + 2] if x_[0] == "kdT"][0][3]
                        pe.wait_ge(free[b_], u_ + 1)
                    wait_free((b, n_))
                    r_ = heads_rows(h)
                    pe.matmul(bank[b][:, 0:W_of(i)], iq3[r_, h // 2, i * P:(i + 1) * P], ikd[r_, 0:W_of(i)],
                              start=True, stop=True).then_inc(full[b], 1)
                if k == "level":
                    _, l, b0, b1 = s
                    B, H = 2 << l, 1 << l
                    pe.wait_ge(S["xm_done"], 2 * (l + 1))
                    xu = hX[l % 2][:, :].rearrange("p (u t) -> p u t", t=C)
                    for q, bu in enumerate((b0, b1)):
                        wait_free(bu)
                        for v in range(8):
                            un = xu[:, 8 * q + v, :]
                            rhs = un.rearrange("p (n b) -> p n b", b=B)[:, :, H:B]
                            ins = pe.matmul(bank[bu[0]][:, 64 * v:64 * v + 64].rearrange("p (n h) -> p n h", h=H), un, rhs,
                                            start=True, stop=True)
                        ins.then_inc(full[bu[0]], 1)
                if k == "diag":
                    for q, bu in enumerate(s[1]):
                        wait_free(bu)
                        for v in range(4):
                            un = 4 * q + v
                            ins = pe.matmul(bank[bu[0]][:, v * P:(v + 1) * P], hk_u[:, un, :], hq_u[:, un, :],
                                            start=True, stop=True)
                        ins.then_inc(full[bu[0]], 1)
                if k == "chunk":
                    _, c, bk, bo, bs = s
                    if c == 0:
                        pe.wait_ge(S["kk_done"], 1)
                        pe.wait_ge(S["qd_done"], 1)
                        for b, u in diag_banks:
                            pe.wait_ge(free[b], u + 1)
                        for b, u in tiles[n_hi + 3]:
                            pe.wait_ge(free[b], u + 1)
                    if c < NT - 1:
                        transposes(bk, [hk_u[:, h * NT + c, :] for h in range(HG)])
                    wait_free(bo)
                    if c:
                        b, u = rec[c - 1][4]
                        pe.wait_ge(free[b], u + 1)
                    for h in range(HG):
                        un = h * NT + c
                        dst = bank[bo[0]][:, h * P:(h + 1) * P]
                        ins = pe.matmul(dst, ha_u[:, un, :], hV3[:, c, h * P:(h + 1) * P], start=True, stop=c == 0)
                        if c:
                            ins = pe.matmul(dst, hq_u[:, un, :], hS[:, h * P:(h + 1) * P], start=False, stop=True)
                    ins.then_inc(full[bo[0]], 1)
                    if c < NT - 1:
                        pe.wait_ge(free[bk[0]], bk[1] + 1)
                        wait_free(bs)
                        for h in range(HG):
                            ins = pe.matmul(bank[bs[0]][:, h * P:(h + 1) * P], hKT[:, h * P:(h + 1) * P],
                                            hV3[:, c, h * P:(h + 1) * P], start=True, stop=True)
                        ins.then_inc(full[bs[0]], 1)
                if k == "oaT":
                    pe.wait_ge(S["on_done"], 16)
                    for h in range(HG):
                        transposes(s[1][h], [hO3[:, t, h * P:(h + 1) * P] for t in range(NT)])
                if k == "flip":
                    pe.wait_ge(S["bt_in"], 16)
                    for h in range(AH):
                        wait_free(flips[h])
                        pe.matmul(bank[flips[h][0]][:, :], flip, bt3[:, h, :], start=True,
                                  stop=True).then_inc(full[flips[h][0]], 1)
                if k == "attn":
                    _, u, bq, btp, bv = s
                    if u < NU:
                        i, h = units[u]
                        if u == 0:
                            for q in range(4):
                                b_, u_ = tiles[n_uq][q]
                                pe.wait_ge(free[b_], u_ + 1)
                            for q in (1, 2):
                                b_, u_ = [x_ for x_ in side[n_hf + 2] if x_[0] == "kdT"][0][q]
                                pe.wait_ge(free[b_], u_ + 1)
                        wait_free(bq)
                        r_ = heads_rows(h)
                        pe.matmul(bank[bq[0]][:, 0:W_of(i)], aq3[r_, h // 2, i * P:(i + 1) * P],
                                  kdup3[r_, h // 4, 0:W_of(i)], start=True, stop=True).then_inc(full[bq[0]], 1)
                    if btp is not None:
                        v = u - 1
                        i, h = units[v]
                        pe.wait_ge(S["e_done"], v + 1)
                        transposes(btp, [tt[v % 2][:, q * P:(q + 1) * P] for q in range(i + 1)])
                    if bv is not None:
                        v = u - 2
                        i, h = units[v]
                        b6 = att[v + 1][3]
                        pe.wait_ge(free[6], b6[1] + 1)
                        wait_free(bv)
                        g = h // 4
                        for q in range(i + 1):
                            ins = pe.matmul(bank[7][:, 0:DH], et[v % 2][:, q * P:(q + 1) * P],
                                            c03[:, q, QL + GR * DH + g * DH:QL + GR * DH + (g + 1) * DH],
                                            start=q == 0, stop=q == i)
                        ins.then_inc(full[7], 1)
                if k == "obT":
                    pe.wait_ge(free[7], att[-1][4][1] + 1)
                    for q in range(4):
                        transposes(s[1][q], [ob3[:, t, q * P:(q + 1) * P] for t in range(NT)])

            for n in range(NPLAN):
                mms(n)
                for s in side[n]:
                    do_side(s)


            pe.wait_ge(S["xn_done"], 2 * NT)
            for k in range(KD_):
                transposes(mlp_bank[k], [ys3[:, t, k * P:(k + 1) * P] for t in range(NT)])
            for b, u in mlp_bank:
                pe.wait_ge(free[b], u + 1)

            def block_(it, last):
                for m in range(PER_FB):
                    n = NPLAN + m
                    s = n % SLOTS
                    pe.wait_ge(lo_done, it * PER_FB + (n + 1))
                    if m < 4:
                        wh, wl = slab_view(whi, s, KD_), slab_view(wlo, s, KD_)
                        pe.wait_ge(free[m], it * 2 + MB)
                        for k in range(KD_):
                            ins = three(bank[m][:, :], wh[:, k, :], wl[:, k, :], hTh3[:, k, :], hTl3[:, k, :],
                                        k == 0, k == KD_ - 1)
                        ins.then_inc(full[m], 1)
                    else:
                        wh, wl = slab_view(whi, s, 2), slab_view(wlo, s, 2)
                        first, k0 = m % 2 == 0, 2 * (m % 2)
                        for kk in range(2):
                            k = k0 + kk
                            if m < 6:
                                pe.wait_ge(S["hl_done"], it * 4 + (k + 1))
                            for t in range(NT):
                                b = 4 + t if m < 6 else t
                                if first and kk == 0:
                                    pe.wait_ge(free[b], it + MB2[t] if m < 6 else it * 2 + (MB + 1))
                                ins = three(bank[b][:, :], hh3[:, k, t * P:(t + 1) * P], hl3[:, k, t * P:(t + 1) * P],
                                            wh[:, kk, :], wl[:, kk, :], first and kk == 0, k == 3)
                                if k == 3:
                                    ins.then_inc(full[b], 1)
                        if first:
                            ins.then_inc(slab_used, 1)

            loop_blocks(pe, block_)


def constants():
    p = np.arange(P)
    k = np.zeros((P, K_COLS), np.float32)
    k[:, K_IDENT:K_IDENT + P] = np.eye(P)
    for l in range(LEVELS):
        half, width = 1 << l, 2 << l
        t = np.arange(P)
        right = t[t % width >= half]
        same = (p[:, None] // width == right[None, :] // width) & (p[:, None] % width < half)
        k[:, K_MASK + 64 * l:K_MASK + 64 * l + 64] = same
    k[:, K_RESET:K_RESET + T] = (np.arange(T) % C != 0)
    k[:, K_CAUSAL:K_CAUSAL + P] = np.where(p[None, :] <= p[:, None], 0.0, NEG)
    k[:, K_FLIP:K_FLIP + P] = np.eye(P)[::-1]
    dist = np.maximum(T - 1 - np.arange(BT_LEN), 0)
    exact, reach = BUCKETS // 2, 128
    large = exact + (np.log(np.maximum(dist, 1).astype(np.float32) / exact) / np.log(reach / exact)
                     * (BUCKETS - exact)).astype(np.int32)
    bucket = np.where(dist < exact, dist, np.minimum(large, BUCKETS - 1))
    onehot = (bucket[None, :] == np.arange(BUCKETS)[:, None]).astype(np.float32)
    return k, onehot


def kernel(x, attn_norm_g, w_in, hgrn_lb_logits, hgrn_norm_g, w_up_hgrn, q_norm_g, w_uq, w_iq, idx_k_norm_g,
           idx_k_norm_b, rel_bias, w_up_attn, w_o, mlp_norm_g, w_mlp_in, w_mlp_out, final_norm_g):
    import concourse.bacc as _bacc
    from concourse.bass_utils import run_bass_kernel_spmd as _run

    A = np.ascontiguousarray

    def slab(w):
        k, c = w.shape[0] // P, w.shape[1]
        s = np.asarray(w).reshape(k, P, c).transpose(1, 0, 2).reshape(P, k * c)
        return s if k * c == SLAB else np.pad(s, ((0, 0), (0, SLAB - k * c)))

    wi = np.asarray(w_in)[0]
    widths = (HGW, HGW, HGW, HGW, QL, GR * DH, GR * DH, DH, IH, D, D)
    o = np.cumsum((0,) + widths)
    q0, f0, i0, g0, c0, ik0, ga0, gb0 = o[0], o[1], o[2], o[3], o[4], o[7], o[9], o[10]
    up_h, up_a, wo = (np.asarray(w)[0] for w in (w_up_hgrn, w_up_attn, w_o))
    uq, iq = np.asarray(w_uq)[0], np.asarray(w_iq)[0]
    m_in, m_out = np.asarray(w_mlp_in)[0], np.asarray(w_mlp_out)[0]
    by_token = {"c0": c0, "hi": i0, "hg": g0}
    by_feature = {"hf": f0, "hq": q0, "ga": ga0, "gb": gb0}
    parts = []
    for kind, j in PLAN:
        if kind in by_token:
            parts.append(wi[2 * P * j:2 * P * (j + 1), by_token[kind]:by_token[kind] + 512])
        elif kind in by_feature:
            parts.append(wi[:, by_feature[kind] + P * j:by_feature[kind] + P * (j + 1)])
        elif kind == "c1":
            parts.append(wi[:, ik0:ik0 + DH + IH])
        elif kind in ("iq", "uq"):
            parts.append(iq if kind == "iq" else uq)
        elif kind in ("ua", "ub"):
            parts.append((up_h if kind == "ua" else up_a)[:, 2 * P * j:2 * P * (j + 1)])
        else:
            parts.append(wo[2 * P * (j % 4):2 * P * (j % 4 + 1), 512 * (j // 4):512 * (j // 4 + 1)])
    for f in range(0, F, FB):
        parts += [m_in[:, f + P * j:f + P * (j + 1)] for j in range(4)]
        parts += [m_out[f + 2 * P * j:f + 2 * P * (j + 1), 512 * h:512 * (h + 1)] for h in range(2) for j in range(2)]
    slabs = A(np.stack([slab(w) for w in parts]))

    def cols(v):
        return np.asarray(v).reshape(-1, P).T

    lbl = np.asarray(hgrn_lb_logits)
    two = lambda v: np.concatenate([np.asarray(v)[0]] * 2).reshape(1, P).T
    vecs = A(np.concatenate([cols(attn_norm_g), cols(mlp_norm_g), cols(q_norm_g), cols(hgrn_norm_g), cols(lbl[0]),
                             cols(lbl[1]), two(idx_k_norm_g), two(idx_k_norm_b)], axis=1))
    k, onehot = constants()
    arrays = {"x": A(np.asarray(x)), "slabs": slabs, "vecs": vecs, "consts": k, "onehot": onehot,
              "rel_bias": A(np.asarray(rel_bias)), "final_g": A(np.asarray(final_norm_g))}
    nc = _bacc.Bacc("TRN2", target_bir_lowering=False, num_devices=1)
    args = [nc.dram_tensor(n, a.shape, mybir.dt.from_np(a.dtype), kind="ExternalInput").ap() for n, a in arrays.items()]
    out = nc.dram_tensor("out", (1, T, D), F32, kind="ExternalOutput").ap()
    build(nc, *args, out)
    r = _run(nc, [arrays], core_ids=[0])
    return r.results[0]["out"]
```

```python
from contextlib import ExitStack

import numpy as np

import concourse.bass as bass
from concourse import mybir

F32 = mybir.dt.float32
F32R = mybir.dt.float32r
I32 = mybir.dt.int32
ALU = mybir.AluOpType
ACT = mybir.ActivationFunctionType
AX = mybir.AxisListType

P = 128
T = 512
D = 1024
NT = T // P
KD_ = D // P
HG = 4
HGW = HG * P
C = P
LEVELS = 7
AH, DH = 8, 64
GR = 2
QL = 256
IH = 8
TOPK = 128
BUCKETS = 32
F = 4 * D
EPS = 1e-6
NEG = -1.0e30
FILL = -3.0e38
TAKEN = -3.4e38
SLAB = 1024
SLOTS = 4
AHEAD = 3

PLAN = ([("hf", j) for j in range(4)] + [("hq", j) for j in range(4)] + [("c0", j) for j in range(4)]
        + [("c1", 0)] + [("hi", j) for j in range(4)] + [("iq", 0), ("uq", 0)]
        + [("hg", j) for j in range(4)] + [("ga", j) for j in range(8)] + [("ua", j) for j in range(4)]
        + [("gb", j) for j in range(8)] + [("ub", j) for j in range(4)] + [("wo", j) for j in range(8)])
NPLAN = len(PLAN)
FB = 512
NFB = F // FB
PER_FB = 8
NSLAB = NPLAN + NFB * PER_FB
AT_SLAB = {k: n for n, k in reversed(list(enumerate(PLAN)))}

K_IDENT, K_MASK, K_RESET, K_CAUSAL = 0, P, P + LEVELS * 64, P + LEVELS * 64 + T
K_FLIP = K_CAUSAL + P
K_COLS = K_FLIP + P
V_ATTN, V_MLP, V_Q, V_HG, V_LB0, V_LB1, V_IKG, V_IKB = 0, 8, 16, 18, 22, 26, 30, 31
V_COLS = 32
WIN = 2 * P
BT_LEN = P + WIN


def build(nc, x, slabs, vecs, consts, onehot, rel_bias, final_g, out):
    with ExitStack() as ctx:
        at = [0]
        base = 16512

        def place(name, off_kb, cols, dt=F32, rows=P):
            return nc.alloc_sbuf_tensor_at(name, [rows, cols], dt, offset=base + int(off_kb * 1024))

        def sem(name):
            return ctx.enter_context(nc.semaphore(name))

        raw = [place(f"raw{s}", 4 * s, SLAB) for s in range(SLOTS)]
        whi = [place(f"whi{s}", 16 + 4 * s, SLAB, F32R) for s in range(SLOTS)]
        wlo = [place(f"wlo{s}", 32 + 4 * s, SLAB, F32R) for s in range(SLOTS)]
        hTh = place("hTh", 48, KD_ * T, F32R)
        hTl = place("hTl", 64, KD_ * T, F32R)
        cst = place("cst", 80, K_COLS)
        vec = place("vec", 85.25, V_COLS)
        small = place("small", 85.5, 256)
        iks = place("iks", 86.5, NT * 72)
        aq = place("aq", 88, 4 * T)
        kdup = place("kdup", 96, GR * T)
        c0s = place("c0s", 100, NT * 512)
        sc = place("sc", 108, 1280)
        hF = place("hF", 113, HG * T)
        hK = place("hK", 121, HG * T)
        hQ = place("hQ", 129, HG * T)
        hV = place("hV", 137, NT * HGW)
        hSG = place("hSG", 145, NT * HGW)
        hX = [place(f"hX{i}", 153 + 8 * i, HG * T) for i in range(2)]
        hA = place("hA", 169, HG * T)
        hS = place("hS", 177, HG * P)
        hKT = place("hKT", 179, HG * P)
        tha = place("tha", 181, KD_ * T)
        xs = place("xs", 113, NT * D)
        cqh = place("cqh", 145, 2 * T, F32R)
        cql = place("cql", 149, 2 * T, F32R)
        kd = place("kd", 137, NT * GR * P)
        ikn = place("ikn", 141, NT * P)
        iq = place("iq", 181, 4 * T)
        ikd = place("ikd", 189, T)
        ikT = place("ikT", 191, T, rows=DH + IH)
        rel = [place(f"rel{i}", 191 + 2 * i, T) for i in range(2)]
        rbias = place("rbias", 195, BT_LEN, rows=AH)
        oneh = place("oneh", 197.5, BT_LEN, rows=BUCKETS)
        rb = place("rb", 200, AH, rows=BUCKETS)
        hO = place("hO", 113, NT * HGW)
        oah = place("oah", 153, HG * T, F32R)
        oal = place("oal", 161, HG * T, F32R)
        bt = place("bt", 129, AH * WIN)
        ob = place("ob", 145, NT * 512)
        bm = [place(f"bm{i}", 169 + 2 * i, T) for i in range(2)]
        tt = [place(f"tt{i}", 173 + 2 * i, T) for i in range(2)]
        tt.append(place("tt2", 197.5, T))
        et = [place(f"et{i}", 177 + 2 * i, T) for i in range(2)]
        obh = place("obh", 113, 4 * T, F32R)
        obl = place("obl", 121, 4 * T, F32R)
        thb = place("thb", 153, KD_ * T)
        mxh = place("mxh", 88, KD_ * T, F32R)
        mxl = place("mxl", 129, KD_ * T, F32R)
        y = place("y", 153, NT * D)
        ys = place("ys", 113, NT * D)
        hh = place("hh", 169, 4 * T, F32R)
        hl = place("hl", 177, 4 * T, F32R)
        rt = [place(f"rt{i}", 185 + 2 * i, T) for i in range(2)]
        hv = [place(f"hv{i}", 189 + 2 * i, T) for i in range(2)]
        fg = place("fg", 193, D)
        junk = place("junk", 202.5, 1024)

        ssx, rsx = small[:, 0:4], small[:, 4:8]
        ssq, rsq = small[:, 8:12], small[:, 12:16]
        mv, rik = small[:, 16:24], small[:, 24:28]
        wix = small[:, 28:60]
        lb, oml = small[:, 60:64], small[:, 64:68]
        ghg = small[:, 68:72]
        sso, rso = small[:, 72:88], small[:, 88:104]
        nmx, esum = small[:, 104:136], small[:, 136:168]
        mx8 = small[:, 168:192]
        bst = small[:, 192:216]
        mhalf = small[:, 216:220]
        lbd = small[:, 220:224]
        resum = small[:, 224:226]
        ssy, rsy = small[:, 226:230], small[:, 230:234]
        ssf, rsf = small[:, 234:238], small[:, 238:242]
        ssg, r2y = small[:, 242:246], small[:, 246:250]

        ident = cst[:, K_IDENT:K_IDENT + P]
        reset = cst[:, K_RESET:K_RESET + T]
        causal = cst[:, K_CAUSAL:K_CAUSAL + P]
        flip = cst[:, K_FLIP:K_FLIP + P]

        bank = [ctx.enter_context(nc.psum_tensor(f"bank{b}", [P, 512], F32)) for b in range(8)]
        scratch = nc.dram_tensor("bias_rows", [AH, BT_LEN], F32).ap()

        raw_in = [sem(f"raw_in{s}") for s in range(SLOTS)]
        hi_done, lo_done, slab_used = sem("hi_done"), sem("lo_done"), sem("slab_used")
        full = [sem(f"full{b}") for b in range(8)]
        free = [sem(f"free{b}") for b in range(8)]
        const_in, fg_in, y_in, out_done = sem("const_in"), sem("fg_in"), sem("y_in"), sem("out_done")
        ident_in, vec_in = sem("ident_in"), sem("vec_in")
        x_in = [sem(f"x_in{t}") for t in range(NT)]
        names = ("sq_done rs_done xn_done hTh_done cqn_done kd_done stat_done mv_done ikn_done wix_done "
                 "cqh_done acc_done causal_done max_done rep_done am_done lbd_done lbs_done lb_done ghg_done "
                 "f_done k_done ln_done scan_done th_done diff_done ex_done xm_done a_zero d0_done d1_done "
                 "e1_done qd_done kk_done ro_done on_done oah_done scr_done bt_in bm_done e_done "
                 "rsum_done obh_done mix_done mxh_done mxl_done hv_done hh_done hl_done fin_done rq_done "
                 "rik_done ry_done rf_done pool_step")
        S = {n: sem(n) for n in names.split()}
        SQ_X, SQ_CQ, SQ_HG, SQ_Y, SQ_F = 0, NT, 2 * NT, 2 * NT + 4 * HG, 3 * NT + 4 * HG

        side = {n: [] for n in range(NPLAN)}
        uses = [0] * 8

        def take(b):
            uses[b] += 1
            return b, uses[b] - 1

        tiles = {}
        for n, (kind, j) in enumerate(PLAN):
            if kind in ("c0", "hi", "hg") and j == 0 or kind == "wo" and j % 4 == 0:
                tiles[n] = [None] * NT
            elif kind in ("c0", "hi", "hg", "wo"):
                tiles[n] = n - 1 if isinstance(tiles[n - 1], list) else tiles[n - 1]
            elif kind == "c1":
                tiles[n] = "side"
            elif kind in ("hf", "hq", "ga", "gb"):
                tiles[n] = [None]
            elif kind in ("iq", "uq"):
                tiles[n] = [None] * 4
            else:
                tiles[n] = [None] * 2
        r = 0
        proj_use = [0] * 4
        for n in range(NPLAN):
            if isinstance(tiles[n], list):
                for q in range(len(tiles[n])):
                    b = r % 4
                    tiles[n][q] = (b, proj_use[b])
                    proj_use[b] += 1
                    r += 1
        for n in range(NPLAN):
            if isinstance(tiles[n], int):
                tiles[n] = tiles[tiles[n]]
        PRO = 1
        tiles = {n: v if v == "side" else [(b, u + PRO) for b, u in v] for n, v in tiles.items()}
        uses[4:8] = [PRO] * 4

        SIDEB = [4, 5, 6, 7]
        rot = [0]

        def nextb():
            b = SIDEB[rot[0] % 4]
            rot[0] += 1
            return take(b)

        n_c0, n_c1, n_hf, n_iq, n_uq = (AT_SLAB[k, 0] for k in ("c0", "c1", "hf", "iq", "uq"))
        n_hq, n_hi, n_hg, n_ga, n_ua, n_gb, n_ub, n_wo = (
            AT_SLAB[k, 0] for k in ("hq", "hi", "hg", "ga", "ua", "gb", "ub", "wo"))
        units = [(i, h) for i in range(NT) for h in range(AH)]
        NU = len(units)
        idx_units = [(i, h) for i in (1, 2, 3) for h in range(IH)]
        rounds = TOPK // 8

        def spread(steps, first, last):
            span = last - first + 1
            for q, s in enumerate(steps):
                side[first + q * span // len(steps)].append(s)

        def file(n, *steps):
            side[n].extend(steps)

        file(n_hf + 2, ("bias_rows",))
        file(n_hq, ("log", 0), ("log", 1))
        file(n_hq + 1, ("log", 2), ("log", 3))
        file(n_hq + 2, ("diff", 0))
        file(n_hq + 3, ("diff", 1))
        n_lv = n_hq + 4
        for l in range(LEVELS):
            file(n_lv + l, ("mul", l))
            if 2 <= l + 1 < LEVELS:
                file(n_lv + l, ("diff", l + 1))
            if l:
                file(n_lv + l, ("put", l - 1))
        L_DIAG = 2
        file(n_lv + L_DIAG, ("diag",))
        file(n_lv + L_DIAG + 1, ("dput",))
        n_de = n_lv + LEVELS
        file(n_de - 1, ("decay_k",))
        file(n_de, ("put", LEVELS - 1), ("use_k",), ("decay_q",))
        file(n_de + 1, ("use_q",))
        file(n_hi, ("ikT",))
        file(n_hi + 1, ("prep",))
        file(n_hi + 2, ("cqT",))
        file(n_hi + 3, ("kdT",))
        n_ch = n_hi + 4
        for c in range(NT):
            if c < NT - 1:
                file(n_ch + c, ("kT", c))
            if c < NT - 1:
                file(n_ch + c + 1, ("state", c))
            file(n_ch + c + 1, ("out", c))
        spread([("index", u, i, h) for u, (i, h) in enumerate(idx_units)], n_uq, n_hg + 3)
        file(n_hg + 3, ("bt", ))
        file(n_ga, *[("on", c) for c in range(NT)])
        spread([("flip", h) for h in range(AH // 2)], n_ga + 1, n_ga + 4)
        file(n_ga + 3, ("oaT",))
        spread([("attn", u) for u in range(NU + 3)], n_ga + 5, n_gb + 5)
        spread([("top", (1, 2), r_) for r_ in range(rounds)], n_hg + 3, n_ga + 5)
        file(n_ga, ("mask", 0))
        file(n_ga + 6, ("mask", 1), ("mask", 2))
        spread([("top", (3,), r_) for r_ in range(rounds)], n_ga + 6, n_gb)
        file(n_gb, ("mask", 3))
        file(n_gb + 6, ("obT",))

        EARLY = (n_iq, n_uq, n_hg + 3)
        need = {"bias_rows": 1, "ikT": 1, "cqT": 2, "kdT": 3, "index": 1, "mul": 2, "diag": 4, "kT": 1, "out": 1, "state": 1,
                "oaT": 4, "flip": 1, "obT": 4}
        BK = {}
        top_at, n_top = {}, 0
        for n in range(NPLAN):
            if n == n_c1:
                c1_bank = nextb()
            for s in side[n]:
                if s[0] == "attn":
                    u = s[1]
                    BK[s] = (take(4 + u % 2) if u < NU else None, take(6) if 2 <= u <= NU + 1 else None,
                             take(7) if u >= 3 else None)
                elif s[0] in need:
                    BK[s] = [nextb() for _ in range(need[s[0]])]
                elif s[0] == "top":
                    for i in s[1]:
                        top_at[i, s[2]] = n_top
                        n_top += 1
        N_TOP = n_top
        mlp_bank = [(b, PRO + proj_use[b] if b < 4 else uses[b]) for b in range(8)]
        assert len({PRO + v for v in proj_use}) == 1
        MLP_K = [4, 0, 5, 6, 7, 1, 2, 3]
        MB = PRO + proj_use[0] + 1
        MB2 = [uses[4 + t] + 1 for t in range(NT)]

        by_count, seen = {}, 0
        for n, (kind, j) in enumerate(PLAN):
            if kind in ("c0", "hi", "hg", "wo") and j % 4 != 3:
                seen += 1
                by_count[n] = seen
        BY_COUNT = seen

        def used_up(n, it=None):
            if it is not None:
                m = n - NPLAN
                if m in (4, 6):
                    return slab_used, it * 2 + (BY_COUNT + m // 2 - 1)
                if m == 5:
                    return full[7], it + (MB2[3] + 1)
                if m in (-1, 7):
                    return full[3], it * 2 + (MB if m == -1 else MB + 2)
                return full[m], it * 2 + (MB + 1)
            if n in by_count:
                return slab_used, by_count[n]
            b, u = c1_bank if tiles[n] == "side" else tiles[n][-1]
            return full[b], u + 1

        def loop_blocks(eng, body):
            with eng.Fori(0, NFB - 1, 1) as it:
                body(it, False)
            body(NFB - 1, True)

        OUT_PARTS = [[slice(0, D)]] * (NT - 1) + [[slice(0, D // 2), slice(D // 2, D)]]

        def W_of(i):
            return (i + 1) * P

        SC_OFF = [0, 128, 384, 768]

        def sc_of(i):
            return sc[:, SC_OFF[i]:SC_OFF[i] + W_of(i)]

        def heads_rows(h):
            return slice(64 * (h % 2), 64 * (h % 2) + 64)

        def slab_view(t, s, kt):
            return t[s][:, :].rearrange("p (k c) -> p k c", k=kt)

        hTh3 = hTh[:, :].rearrange("p (k t) -> p k t", k=KD_)
        hTl3 = hTl[:, :].rearrange("p (k t) -> p k t", k=KD_)
        cqh3 = cqh[:, :].rearrange("p (k t) -> p k t", k=2)
        cql3 = cql[:, :].rearrange("p (k t) -> p k t", k=2)
        oah3 = oah[:, :].rearrange("p (k t) -> p k t", k=HG)
        oal3 = oal[:, :].rearrange("p (k t) -> p k t", k=HG)
        obh3 = obh[:, :].rearrange("p (k t) -> p k t", k=4)
        obl3 = obl[:, :].rearrange("p (k t) -> p k t", k=4)
        mxh3 = mxh[:, :].rearrange("p (k t) -> p k t", k=KD_)
        mxl3 = mxl[:, :].rearrange("p (k t) -> p k t", k=KD_)
        hh3 = hh[:, :].rearrange("p (k t) -> p k t", k=4)
        hl3 = hl[:, :].rearrange("p (k t) -> p k t", k=4)
        c03 = c0s[:, :].rearrange("p (t c) -> p t c", t=NT)
        kd5 = kd[:, :].rearrange("p (t g u d) -> p t g u d", t=NT, g=GR, u=2)
        ikn4 = ikn[:, :].rearrange("p (t u d) -> p t u d", t=NT, u=2)
        iks3 = iks[:, :].rearrange("p (t c) -> p t c", t=NT)
        aq3 = aq[:, :].rearrange("p (j t) -> p j t", j=4)
        iq3 = iq[:, :].rearrange("p (j t) -> p j t", j=4)
        kdup3 = kdup[:, :].rearrange("p (g t) -> p g t", g=GR)
        y3 = y[:, :].rearrange("p (t c) -> p t c", t=NT)
        ys3 = ys[:, :].rearrange("p (t c) -> p t c", t=NT)
        xs3 = xs[:, :].rearrange("p (t c) -> p t c", t=NT)
        tha3 = tha[:, :].rearrange("p (m t) -> p m t", m=KD_)
        thb3 = thb[:, :].rearrange("p (m t) -> p m t", m=KD_)
        hV3 = hV[:, :].rearrange("p (t c) -> p t c", t=NT)
        hSG3 = hSG[:, :].rearrange("p (t c) -> p t c", t=NT)
        hO3 = hO[:, :].rearrange("p (t c) -> p t c", t=NT)
        ob3 = ob[:, :].rearrange("p (t c) -> p t c", t=NT)
        bt3 = bt[:, :].rearrange("p (h c) -> p h c", h=AH)
        hq_u = hQ[:, :].rearrange("p (u t) -> p u t", t=C)
        hk_u = hK[:, :].rearrange("p (u t) -> p u t", t=C)
        hf_u = hF[:, :].rearrange("p (u t) -> p u t", t=C)
        ha_u = hA[:, :].rearrange("p (u t) -> p u t", t=C)
        hx0_u = hX[0][:, :].rearrange("p (u t) -> p u t", t=C)
        x_t = x.rearrange("b (t p) d -> (b t) p d", p=P)
        out_t = out.rearrange("b (t p) d -> (b t) p d", p=P)

        block = ctx.enter_context(nc.Block())

        @block.sync
        def _(sp):
            sp.dma_start(ident, consts[:, K_IDENT:K_IDENT + P]).then_inc(ident_in, 16)
            for t in range(NT):
                sp.dma_start(xs3[:, t, :], x_t[t]).then_inc(x_in[t], 16)
            sp.dma_start(vec[:, :], vecs).then_inc(vec_in, 16)

            def load(n, dyn=None):
                s = n % SLOTS
                if n >= SLOTS:
                    sp.wait_ge(lo_done, n - SLOTS + 1 if dyn is None else dyn * PER_FB + (n - SLOTS + 1))
                sp.dma_start(raw[s][:, :], slabs[n] if dyn is None else
                             slabs[bass.ds(dyn * PER_FB + n, 1), :, :].rearrange("a p c -> (a p) c")
                             ).then_inc(raw_in[s], 16)

            for n in range(SLOTS):
                load(n)
            sp.dma_start(cst[:, P:K_COLS], consts[:, P:K_COLS]).then_inc(const_in, 16)
            sp.dma_start(oneh[:, :], onehot).then_inc(const_in, 16)
            sp.dma_start(rb[:, :], rel_bias).then_inc(const_in, 16)
            for n in range(SLOTS, NPLAN):
                load(n)
                if n == n_hf + 8:
                    for b, u in BK["bias_rows",]:
                        sp.wait_ge(free[b], u + 1)
                    sp.dma_start(scratch, rbias[:, :]).then_inc(S["scr_done"], 16)
            sp.wait_ge(S["mxl_done"], KD_)
            sp.dma_start(fg[:, :], final_g.partition_broadcast(P)).then_inc(fg_in, 16)
            with sp.Fori(0, NFB, 1) as it:
                for m in range(PER_FB):
                    load(NPLAN + m, it)
            parts_out = [(t, c) for t in range(NT) for c in OUT_PARTS[t]]
            for q, (t, c) in enumerate(parts_out):
                sp.wait_ge(S["fin_done"], q + 1)
                sp.dma_start(out_t[t][:, c], ys3[:, t, c]).then_inc(out_done, 16)
            sp.wait_ge(out_done, 16 * len(parts_out))

        @block.gpsimd
        def _(pool):
            pg = [0]

            def chain(ins):
                pg[0] += 1
                ins.then_inc(S["pool_step"], 1)
                pool.wait_ge(S["pool_step"], pg[0])

            def rsqrt_mean(dst, src, n, width):
                chain(pool.tensor_scalar(dst, src, 1.0 / width, EPS, ALU.mult, ALU.add))
                return pool.tensor_tensor(dst, dst, mhalf[:, 0:n], ALU.pow)

            chain(pool.memset(mhalf, -0.5))
            pool.memset(hA[:, :], 0.0).then_inc(S["a_zero"], 1)
            for t in range(NT):
                pool.wait_ge(S["sq_done"], SQ_X + t + 1)
                rsqrt_mean(rsx[:, t:t + 1], ssx[:, t:t + 1], 1, D).then_inc(S["rs_done"], 1)

            def do_side(s):
                if s[0] == "prep":
                    pool.wait_ge(S["sq_done"], SQ_CQ + NT)
                    rsqrt_mean(rsq, ssq, NT, QL).then_inc(S["rq_done"], 1)
                    for g in range(GR):
                        src = c03[:, :, QL + DH * g:QL + DH * g + DH].unsqueeze(2).to_broadcast([P, NT, 2, DH])
                        pool.tensor_copy(kd5[:, :, g], src).then_inc(S["kd_done"], 1)
                    pool.wait_ge(S["mv_done"], NT)
                    mv3 = mv.rearrange("p (t c) -> p t c", c=2)
                    rsqrt_mean(rik, mv3[:, :, 1], NT, 1).then_inc(S["rik_done"], 1)
                if s[0] == "index":
                    _, u, i, h = s
                    if h == IH - 1:
                        pool.wait_ge(S["acc_done"], u + 1)
                        q = sc_of(i)[:, i * P:(i + 1) * P]
                        pool.affine_select(out=q, in_=q, compare_op=ALU.is_ge, fill=FILL, base=0,
                                           pattern=[[-1, P]], channel_multiplier=1).then_inc(S["causal_done"], 1)
                if s[0] == "out":
                    c = s[1]
                    pool.wait_ge(S["sq_done"], SQ_HG + HG * (c + 1))
                    rsqrt_mean(rso[:, 4 * c:4 * c + 4], sso[:, 4 * c:4 * c + 4], 4, P).then_inc(S["ro_done"], 1)
                if s[0] == "attn" and s[1] < NU:
                    u = s[1]
                    i, h = units[u]
                    if u == 0:
                        b, n_ = BK["flip", AH // 2 - 1][0]
                        pool.wait_ge(free[b], n_ + 1)
                        b, n_ = BK["out", NT - 1][0]
                        pool.wait_ge(full[b], n_ + 1)
                    if h == 0:
                        pool.wait_ge(S["am_done"], i + 1)
                    if u >= 2:
                        b, n_ = BK["attn", u - 2][0]
                        pool.wait_ge(free[b], n_ + 1)
                    w = W_of(i)
                    far = max(w - WIN, 0)
                    if far:
                        pool.tensor_scalar(bm[u % 2][:, 0:far], sc_of(i)[:, 0:far], bt3[:, h, 0:1], None, ALU.add)
                    pool.tensor_tensor(bm[u % 2][:, far:w], bt3[:, h, WIN - (w - far):WIN], sc_of(i)[:, far:w],
                                       ALU.add).then_inc(S["bm_done"], 1)

            for n in range(NPLAN):
                for s in side[n]:
                    do_side(s)
            pool.wait_ge(S["sq_done"], SQ_Y + NT)
            chain(rsqrt_mean(rsy, ssy, NT, D))
            pool.tensor_tensor(r2y, rsy, rsy, ALU.mult).then_inc(S["ry_done"], 1)
            for t in range(NT):
                pool.wait_ge(S["sq_done"], SQ_F + NT + t + 1)
                c = slice(t, t + 1)
                chain(pool.tensor_tensor(ssf[:, c], ssf[:, c], ssg[:, c], ALU.add))
                rsqrt_mean(rsf[:, c], ssf[:, c], 1, D).then_inc(S["rf_done"], 1)

        @block.scalar
        def _(act):
            def hi(n, it=None):
                s = n % SLOTS
                arrived = 16 * (n // SLOTS + 1)
                act.wait_ge(raw_in[s], arrived if it is None else it * (16 * PER_FB // SLOTS) + arrived)
                if n >= SLOTS:
                    act.wait_ge(*used_up(n - SLOTS, it))
                act.copy(whi[s][:, :], raw[s][:, :]).then_inc(hi_done, 1)

            def wait_full(bu):
                act.wait_ge(full[bu[0]], bu[1] + 1)

            squares = [0]

            def square(src, width, acc):
                if squares[0]:
                    act.wait_ge(S["sq_done"], squares[0])
                squares[0] += 1
                act.activation(junk[:, 0:width], src, ACT.Square, accum_out=acc).then_inc(S["sq_done"], 1)

            for t in range(NT):
                act.wait_ge(x_in[t], 16)
                square(xs3[:, t, :], D, ssx[:, t:t + 1])
            hi(0)
            act.wait_ge(vec_in, 16)
            for k in range(KD_):
                act.wait_ge(full[k], 1)
                act.activation(hTh3[:, k, :], bank[k][:, :], ACT.Copy,
                               scale=vec[:, V_ATTN + k:V_ATTN + k + 1]).then_inc(S["hTh_done"], 1)
            hi(1)
            act.wait_ge(S["lbd_done"], 1)
            act.activation(lb, lbd, ACT.Sigmoid).then_inc(S["lbs_done"], 1)
            hi(2)

            def copy_out(dst, bu, signal, **kw):
                wait_full(bu)
                act.activation(dst, bank[bu[0]][:, :], kw.pop("func", ACT.Copy), **kw).then_inc(S[signal], 1)

            def evict(n):
                kind, j = PLAN[n]
                if kind == "c0" and j == 3:
                    for t in range(NT):
                        b, u = tiles[n][t]
                        wait_full((b, u))
                        act.activation(c03[:, t, :], bank[b][:, :], ACT.Copy).then_inc(free[b], 1)
                    for t in range(NT):
                        b, u = tiles[n][t]
                        act.wait_ge(free[b], u + 1)
                        square(c03[:, t, 0:QL], QL, ssq[:, t:t + 1])
                if kind == "c1":
                    b, u = c1_bank
                    wait_full(c1_bank)
                    act.activation(ikT[:, :], bank[b][0:DH + IH, :], ACT.Copy).then_inc(free[b], 1)
                if kind == "hf":
                    b, u = tiles[n][0]
                    wait_full((b, u))
                    act.activation(hF[:, j * T:(j + 1) * T], bank[b][:, :], ACT.Sigmoid).then_inc(free[b], 1)
                if kind == "iq":
                    for q, (b, u) in enumerate(tiles[n]):
                        wait_full((b, u))
                        act.activation(iq3[:, q, :], bank[b][:, :], ACT.Copy).then_inc(free[b], 1)
                if kind == "hq":
                    b, u = tiles[n][0]
                    wait_full((b, u))
                    act.activation(hQ[:, j * T:(j + 1) * T], bank[b][:, :], ACT.Copy).then_inc(free[b], 1)
                if kind == "hi" and j == 3:
                    wait_full(BK["kdT",][2])
                    for t, (b, u) in enumerate(tiles[n]):
                        wait_full((b, u))
                        act.activation(hV3[:, t, :], bank[b][:, :], ACT.Copy).then_inc(free[b], 1)
                if kind == "hg" and j == 3:
                    for t, (b, u) in enumerate(tiles[n]):
                        wait_full((b, u))
                        act.activation(hSG3[:, t, :], bank[b][:, :], ACT.Tanh, scale=0.5).then_inc(S["th_done"], 1)
                if kind == "ga":
                    b, u = tiles[n][0]
                    wait_full((b, u))
                    if j == 0:
                        act.wait_ge(S["acc_done"], len(idx_units))
                        act.wait_ge(S["scr_done"], 16)
                    act.activation(tha3[:, j, :], bank[b][:, :], ACT.Tanh, scale=0.5).then_inc(free[b], 1)
                if kind == "gb":
                    b, u = tiles[n][0]
                    wait_full((b, u))
                    act.activation(thb3[:, j, :], bank[b][:, :], ACT.Tanh, scale=0.5).then_inc(free[b], 1)
                if kind == "ub":
                    for q, (b, u) in enumerate(tiles[n]):
                        m = 2 * j + q
                        act.wait_ge(S["mix_done"], m + 1)
                        act.activation(mxh3[:, m, :], tha3[:, m, :], ACT.Copy).then_inc(S["mxh_done"], 1)
                    if j == 3:
                        act.dma_start(y3[:, :, :], x.rearrange("b (t p) d -> p (b t) d", p=P)).then_inc(y_in, 16)

            def do_side(s):
                k = s[0]
                if k == "ikT":
                    b, u = BK[s][0]
                    wait_full((b, u))
                    act.activation(iks[:, :], bank[b][:, 0:NT * (DH + IH)], ACT.Copy).then_inc(free[b], 1)
                if k == "cqT":
                    for q in range(2):
                        copy_out(cqh3[:, q, :], BK[s][q], "cqh_done", scale=vec[:, V_Q + q:V_Q + q + 1])
                if k == "kdT":
                    for g in range(GR):
                        b, u = BK[s][g]
                        wait_full((b, u))
                        act.activation(kdup3[:, g, :], bank[b][:, :], ACT.Copy).then_inc(free[b], 1)
                if k == "index":
                    _, u, i, h = s
                    b, n_ = BK[s][0]
                    wait_full((b, n_))
                    if u >= 2:
                        act.wait_ge(S["acc_done"], u - 1)
                    act.activation(rel[u % 2][:, 0:W_of(i)], bank[b][:, 0:W_of(i)], ACT.Relu,
                                   scale=DH ** -0.5).then_inc(free[b], 1)
                if k == "log":
                    j = s[1]
                    act.wait_ge(S["k_done"], j + 1)
                    f = hF[:, j * T:(j + 1) * T]
                    act.activation(f, f, ACT.Ln).then_inc(S["ln_done"], 1)
                if k == "diff":
                    l = s[1]
                    act.wait_ge(S["diff_done"], 2 * (l + 1))
                    act.activation(hX[l % 2][:, :], hX[l % 2][:, :], ACT.Exp).then_inc(S["ex_done"], 1)
                if k == "decay_k":
                    act.wait_ge(S["d1_done"], 1)
                    act.activation(hX[1][:, :], hX[1][:, :], ACT.Exp).then_inc(S["e1_done"], 1)
                if k == "decay_q":
                    wait_full(BK["mul", LEVELS - 1][1])
                    act.activation(hX[0][:, :], hF[:, :], ACT.Exp).then_inc(S["d0_done"], 1)
                if k == "kT":
                    c = s[1]
                    bk = BK[s][0]
                    wait_full(bk)
                    if c:
                        wait_full(BK["state", c - 1][0])
                    act.activation(hKT[:, :], bank[bk[0]][:, :], ACT.Copy).then_inc(free[bk[0]], 1)
                if k == "out":
                    c = s[1]
                    bo = BK[s][0]
                    wait_full(bo)
                    if c == 0:
                        act.wait_ge(S["d0_done"], 1)
                        act.wait_ge(S["d1_done"], 1)
                    act.activation(hO3[:, c, :], bank[bo[0]][:, :], ACT.Copy).then_inc(free[bo[0]], 1)
                    act.wait_ge(free[bo[0]], bo[1] + 1)
                    for h in range(HG):
                        q = HG * c + h
                        square(hO3[:, c, h * P:(h + 1) * P], P, sso[:, q:q + 1])
                if k == "bt":
                    wait_full(BK["out", NT - 1][0])
                    act.wait_ge(S["scr_done"], 16)
                    src = bass.AP(tensor=scratch.tensor, offset=0, ap=[[1, P], [BT_LEN, AH], [1, WIN]])
                    act.dma_start(bt3[:, :, :], src).then_inc(S["bt_in"], 16)
                if k == "oaT":
                    b, u = BK["state", NT - 2][0]
                    act.wait_ge(free[b], u + 1)
                    act.wait_ge(S["ghg_done"], 1)
                    for h in range(HG):
                        copy_out(oah3[:, h, :], BK[s][h], "oah_done", scale=ghg[:, h:h + 1])
                if k == "flip":
                    h = s[1]
                    b, u = BK[s][0]
                    wait_full((b, u))
                    act.activation(bt[:, 512 * h:512 * h + 512], bank[b][:, :], ACT.Copy).then_inc(free[b], 1)
                if k == "attn":
                    u = s[1]
                    bq, btp, bv = BK[s]
                    if btp is not None:
                        v = u - 2
                        i, h = units[v]
                        wait_full(btp)
                        if v >= 2:
                            wait_full(BK["attn", v + 1][2])
                        act.activation(et[v % 2][:, 0:W_of(i)], bank[6][:, 0:W_of(i)],
                                       ACT.Copy).then_inc(free[6], 1)
                    if u < NU:
                        i, h = units[u]
                        act.wait_ge(free[bq[0]], bq[1] + 1)
                        w = W_of(i)
                        act.activation(tt[u % 3][:, 0:w], tt[u % 3][:, 0:w], ACT.Exp, scale=-1.0,
                                       bias=nmx[:, u:u + 1], accum_out=esum[:, u:u + 1]).then_inc(S["e_done"], 1)
                if k == "obT":
                    for q in range(4):
                        copy_out(obh3[:, q, :], BK[s][q], "obh_done")

            for n in range(NPLAN):
                hi(n + AHEAD)
                if n in EARLY:
                    evict(n)
                for s in side[n]:
                    do_side(s)
                if n not in EARLY:
                    evict(n)
            for k in MLP_K:
                copy_out(hTh3[:, k, :], mlp_bank[k], "hTh_done", scale=vec[:, V_MLP + k:V_MLP + k + 1])
            for t in range(NT):
                b, u = tiles[n_wo + 7][t]
                act.wait_ge(free[b], u + 1)
                square(y3[:, t, :], D, ssy[:, t:t + 1])

            def block_(it, last):
                for m in range(PER_FB):
                    if not (last and m + AHEAD >= PER_FB):
                        hi(NPLAN + m + AHEAD, it)
                    if m < 4:
                        act.wait_ge(full[m], it * 2 + (MB + 1))
                        act.activation(rt[m % 2][:, :], bank[m][:, :], ACT.Relu).then_inc(free[m], 1)
                        act.wait_ge(S["hv_done"], it * 4 + (m + 1))
                        act.activation(hh3[:, m, :], hv[m % 2][:, :], ACT.Copy).then_inc(S["hh_done"], 1)

            loop_blocks(act, block_)
            for t in range(NT):
                act.wait_ge(free[4 + t], MB2[t] + NFB)
                square(y3[:, t, 0:512], 512, ssf[:, t:t + 1])
            for t in range(NT):
                act.wait_ge(free[t], MB + 2 * NFB)
                square(y3[:, t, 512:D], 512, ssg[:, t:t + 1])

        @block.vector
        def _(dve):
            def lo(n, it=None):
                s = n % SLOTS
                dve.wait_ge(hi_done, n + 1 if it is None else it * PER_FB + (n + 1))
                dve.tensor_tensor(wlo[s][:, :], raw[s][:, :], whi[s][:, :].bitcast(F32),
                                  ALU.subtract).then_inc(lo_done, 1)

            def wait_full(bu):
                dve.wait_ge(full[bu[0]], bu[1] + 1)

            for t in range(NT):
                dve.wait_ge(S["rs_done"], t + 1)
                dve.tensor_scalar(xs3[:, t, :], xs3[:, t, :], rsx[:, t:t + 1], None,
                                  ALU.mult).then_inc(S["xn_done"], 1)
            lo(0)
            dve.wait_ge(vec_in, 16)
            dve.tensor_tensor(lbd, vec[:, V_LB0:V_LB0 + 4], vec[:, V_LB1:V_LB1 + 4],
                              ALU.subtract).then_inc(S["lbd_done"], 1)
            dve.tensor_scalar(ghg, vec[:, V_HG:V_HG + 4], 0.5, None, ALU.mult).then_inc(S["ghg_done"], 1)

            def lo_scaled(dst, bu, scale, hi_ap, hi_sem, val):
                dve.wait_ge(S[hi_sem], val)
                dve.scalar_tensor_tensor(out=dst, in0=bank[bu[0]][:, :], scalar=scale, in1=hi_ap.bitcast(F32),
                                         op0=ALU.mult, op1=ALU.subtract).then_inc(free[bu[0]], 1)

            for k in range(KD_):
                lo_scaled(hTl3[:, k, :], (k, 0), vec[:, V_ATTN + k:V_ATTN + k + 1], hTh3[:, k, :], "hTh_done", k + 1)
            lo(1)
            dve.wait_ge(S["lbs_done"], 1)
            dve.tensor_scalar(oml, lb, -1.0, 1.0, ALU.mult, ALU.add).then_inc(S["lb_done"], 1)
            lo(2)

            def evict(n):
                kind, j = PLAN[n]
                if kind == "hf":
                    b, u = tiles[n][0]
                    f, k = hF[:, j * T:(j + 1) * T], hK[:, j * T:(j + 1) * T]
                    dve.wait_ge(free[b], u + 1)
                    dve.wait_ge(S["lb_done"], 1)
                    dve.tensor_scalar(f, f, oml[:, j:j + 1], lb[:, j:j + 1], ALU.mult, ALU.add).then_inc(S["f_done"], 1)
                    dve.wait_ge(S["f_done"], j + 1)
                    dve.tensor_scalar(k, f, -1.0, 1.0, ALU.mult, ALU.add).then_inc(S["k_done"], 1)
                if kind == "uq":
                    for q, (b, u) in enumerate(tiles[n]):
                        wait_full((b, u))
                        dve.tensor_scalar(aq3[:, q, :], bank[b][:, :], DH ** -0.5, None, ALU.mult).then_inc(free[b], 1)
                if kind == "hg" and j == 3:
                    for t, (b, u) in enumerate(tiles[n]):
                        dve.wait_ge(S["th_done"], t + 1)
                        dve.scalar_tensor_tensor(out=hSG3[:, t, :], in0=hSG3[:, t, :], scalar=1.0, in1=bank[b][:, :],
                                                 op0=ALU.add, op1=ALU.mult).then_inc(free[b], 1)
                if kind == "ua":
                    for q, (b, u) in enumerate(tiles[n]):
                        m = 2 * j + q
                        wait_full((b, u))
                        gb, gu = tiles[n_ga + m][0]
                        dve.wait_ge(free[gb], gu + 1)
                        dve.scalar_tensor_tensor(out=tha3[:, m, :], in0=tha3[:, m, :], scalar=1.0, in1=bank[b][:, :],
                                                 op0=ALU.add, op1=ALU.mult).then_inc(free[b], 1)
                if kind == "ub":
                    for q, (b, u) in enumerate(tiles[n]):
                        m = 2 * j + q
                        wait_full((b, u))
                        gb, gu = tiles[n_gb + m][0]
                        dve.wait_ge(free[gb], gu + 1)
                        dve.scalar_tensor_tensor(out=thb3[:, m, :], in0=thb3[:, m, :], scalar=1.0, in1=bank[b][:, :],
                                                 op0=ALU.add, op1=ALU.mult).then_inc(free[b], 1)
                    for q, (b, u) in enumerate(tiles[n]):
                        m = 2 * j + q
                        dve.wait_ge(free[b], u + 1)
                        dve.tensor_tensor(tha3[:, m, :], tha3[:, m, :], thb3[:, m, :], ALU.add).then_inc(S["mix_done"], 1)
                    for q in range(2):
                        m = 2 * j + q
                        dve.wait_ge(S["mxh_done"], m + 1)
                        dve.tensor_tensor(mxl3[:, m, :], tha3[:, m, :], mxh3[:, m, :].bitcast(F32),
                                          ALU.subtract).then_inc(S["mxl_done"], 1)
                if kind == "wo" and j % 4 == 3:
                    half = j // 4
                    if half == 0:
                        dve.wait_ge(y_in, 16)
                    for t, (b, u) in enumerate(tiles[n]):
                        wait_full((b, u))
                        yy = y3[:, t, half * 512:(half + 1) * 512]
                        dve.scalar_tensor_tensor(out=yy, in0=bank[b][:, :], scalar=0.5, in1=yy,
                                                 op0=ALU.mult, op1=ALU.add).then_inc(free[b], 1)

            def do_side(s):
                k = s[0]
                if k == "bias_rows":
                    b, u = BK[s][0]
                    wait_full((b, u))
                    dve.tensor_copy(rbias[:, :], bank[b][0:AH, 0:BT_LEN]).then_inc(free[b], 1)
                if k == "prep":
                    dve.wait_ge(S["rq_done"], 1)
                    for t in range(NT):
                        q = c03[:, t, 0:QL]
                        dve.tensor_scalar(q, q, rsq[:, t:t + 1], None, ALU.mult).then_inc(S["cqn_done"], 1)
                    b, u = BK["ikT",][0]
                    dve.wait_ge(free[b], u + 1)
                    dve.tensor_scalar(wix.rearrange("p (t h) -> p t h", t=NT), iks3[:, :, DH:DH + IH],
                                      IH ** -0.5, None, ALU.mult).then_inc(S["wix_done"], 1)
                    for t in range(NT):
                        dve.bn_stats(bst[:, 6 * t:6 * t + 6], iks3[:, t, 0:DH]).then_inc(S["stat_done"], 1)
                    for t in range(NT):
                        dve.wait_ge(S["stat_done"], t + 1)
                        dve.bn_aggr(mv[:, 2 * t:2 * t + 2], bst[:, 6 * t:6 * t + 6]).then_inc(S["mv_done"], 1)
                    dve.wait_ge(S["rik_done"], 1)
                    for t in range(NT):
                        dve.tensor_scalar(ikn4[:, t], iks3[:, t, 0:DH].unsqueeze(1).to_broadcast([P, 2, DH]),
                                          mv[:, 2 * t:2 * t + 1], rik[:, t:t + 1], ALU.subtract,
                                          ALU.mult).then_inc(S["ikn_done"], 1)
                if k == "cqT":
                    for q in range(2):
                        lo_scaled(cql3[:, q, :], BK[s][q], vec[:, V_Q + q:V_Q + q + 1], cqh3[:, q, :], "cqh_done", q + 1)
                if k == "kdT":
                    b, u = BK[s][2]
                    wait_full((b, u))
                    dve.tensor_scalar(ikd[:, :], bank[b][:, :], vec[:, V_IKG:V_IKG + 1], vec[:, V_IKB:V_IKB + 1],
                                      ALU.mult, ALU.add).then_inc(free[b], 1)
                if k == "index":
                    _, u, i, h = s
                    b, n_ = BK[s][0]
                    dve.wait_ge(free[b], n_ + 1)
                    w = wix[:, i * IH + h:i * IH + h + 1]
                    r_ = rel[u % 2][:, 0:W_of(i)]
                    if h == 0:
                        dve.tensor_scalar(sc_of(i), r_, w, None, ALU.mult).then_inc(S["acc_done"], 1)
                    else:
                        dve.wait_ge(S["acc_done"], u)
                        dve.scalar_tensor_tensor(out=sc_of(i), in0=r_, scalar=w, in1=sc_of(i), op0=ALU.mult,
                                                 op1=ALU.add).then_inc(S["acc_done"], 1)
                if k == "top":
                    _, tiles_, r_ = s
                    for i in tiles_:
                        if r_ == 0:
                            dve.wait_ge(S["causal_done"], i)
                        else:
                            dve.wait_ge(S["rep_done"], top_at[i, r_ - 1] + 1)
                        dve.max(mx8[:, 8 * (i - 1):8 * i], sc_of(i)).then_inc(S["max_done"], 1)
                    for i in tiles_:
                        dve.wait_ge(S["max_done"], top_at[i, r_] + 1)
                        dve.match_replace(sc_of(i), mx8[:, 8 * (i - 1):8 * i], sc_of(i), TAKEN).then_inc(S["rep_done"], 1)
                if k == "mask":
                    i = s[1]
                    if i == 0:
                        dve.tensor_copy(sc_of(0), causal).then_inc(S["am_done"], 1)
                    else:
                        dve.wait_ge(S["rep_done"], top_at[i, rounds - 1] + 1)
                        dve.tensor_scalar(sc_of(i), sc_of(i), (FILL + TAKEN) / 2, NEG, ALU.is_gt,
                                          ALU.mult).then_inc(S["am_done"], 1)
                if k == "log":
                    j = s[1]
                    dve.wait_ge(const_in, 48)
                    dve.wait_ge(S["ln_done"], j + 1)
                    f = hF[:, j * T:(j + 1) * T]
                    dve.tensor_tensor_scan(f, reset, f, 0.0, ALU.mult, ALU.add).then_inc(S["scan_done"], 1)
                if k == "diff":
                    l = s[1]
                    B, H = 2 << l, 1 << l
                    dve.wait_ge(S["scan_done"], HG)
                    if l >= 2:
                        wait_full(BK["mul", l - 2][1])
                    f = hF[:, :].rearrange("p (n b) -> p n b", b=B)
                    xx = hX[l % 2][:, :].rearrange("p (n b) -> p n b", b=B)
                    mid = f[:, :, H - 1:H].to_broadcast([P, HG * T // B, H])
                    dve.tensor_tensor(xx[:, :, H:B], f[:, :, H:B], mid, ALU.subtract).then_inc(S["diff_done"], 1)
                    dve.tensor_tensor(xx[:, :, 0:H], mid, f[:, :, 0:H], ALU.subtract).then_inc(S["diff_done"], 1)
                if k == "mul":
                    l = s[1]
                    B, H = 2 << l, 1 << l
                    xx = hX[l % 2][:, :].rearrange("p (n b) -> p n b", b=B)
                    q3 = hQ[:, :].rearrange("p (n b) -> p n b", b=B)
                    k3 = hK[:, :].rearrange("p (n b) -> p n b", b=B)
                    dve.wait_ge(S["ex_done"], l + 1)
                    if l == 0:
                        for q_ in range(4):
                            b_, u_ = tiles[n_hq + q_][0]
                            dve.wait_ge(free[b_], u_ + 1)
                    dve.tensor_tensor(xx[:, :, H:B], xx[:, :, H:B], q3[:, :, H:B], ALU.mult).then_inc(S["xm_done"], 1)
                    dve.tensor_tensor(xx[:, :, 0:H], xx[:, :, 0:H], k3[:, :, 0:H], ALU.mult).then_inc(S["xm_done"], 1)
                if k == "put":
                    l = s[1]
                    B, H = 2 << l, 1 << l
                    if l == 0:
                        dve.wait_ge(S["a_zero"], 1)
                    mask = cst[:, K_MASK + 64 * l:K_MASK + 64 * l + 64].rearrange("p (n h) -> p n h", h=H)
                    mask = mask.unsqueeze(1).to_broadcast([P, 8, C // B, H]).bitcast(I32)
                    for q, bu in enumerate(BK["mul", l]):
                        if l:
                            last = BK["diag",] if l == L_DIAG + 1 else BK["mul", l - 1]
                            for b_, u_ in last:
                                dve.wait_ge(free[b_], u_ + 1)
                        wait_full(bu)
                        dst = ha_u[:, 8 * q:8 * q + 8, :].rearrange("p u (n b) -> p u n b", b=B)[:, :, :, H:B]
                        src = bank[bu[0]][:, :].rearrange("p (u n h) -> p u n h", u=8, h=H)
                        dve.copy_predicated(dst, mask, src).then_inc(free[bu[0]], 1)
                if k == "dput":
                    mask = ident.unsqueeze(1).to_broadcast([P, 4, C]).bitcast(I32)
                    b, u = BK["mul", L_DIAG][1]
                    dve.wait_ge(free[b], u + 1)
                    for q, bu in enumerate(BK["diag",]):
                        wait_full(bu)
                        dve.copy_predicated(ha_u[:, 4 * q:4 * q + 4, :], mask,
                                            bank[bu[0]][:, :].rearrange("p (u t) -> p u t", u=4)).then_inc(free[bu[0]], 1)
                if k == "decay_k":
                    wait_full(BK["mul", LEVELS - 2][1])
                    dve.tensor_tensor(hX[1][:, :].rearrange("p (u t) -> p u t", t=C),
                                      hf_u[:, :, C - 1:C].to_broadcast([P, 16, C]), hf_u[:, :, :],
                                      ALU.subtract).then_inc(S["d1_done"], 1)
                if k == "use_k":
                    wait_full(BK["diag",][3])
                    dve.wait_ge(S["xm_done"], 2 * LEVELS)
                    dve.wait_ge(S["e1_done"], 1)
                    dve.tensor_tensor(hK[:, :], hK[:, :], hX[1][:, :], ALU.mult).then_inc(S["kk_done"], 1)
                if k == "use_q":
                    dve.wait_ge(S["d0_done"], 1)
                    dve.tensor_tensor(hQ[:, :], hQ[:, :], hX[0][:, :], ALU.mult).then_inc(S["qd_done"], 1)
                if k == "state":
                    c = s[1]
                    bs = BK[s][0]
                    wait_full(bs)
                    for h in range(HG):
                        st = hS[:, h * P:(h + 1) * P]
                        ps = bank[bs[0]][:, h * P:(h + 1) * P]
                        if c == 0:
                            ins = dve.tensor_copy(st, ps)
                        else:
                            b, u = BK["out", c][0]
                            dve.wait_ge(full[b], u + 1)
                            dec = hx0_u[:, h * NT + c, C - 1:C]
                            ins = dve.scalar_tensor_tensor(out=st, in0=st, scalar=dec, in1=ps, op0=ALU.mult,
                                                           op1=ALU.add)
                    ins.then_inc(free[bs[0]], 1)
                if k == "on":
                    c = s[1]
                    dve.wait_ge(S["ro_done"], c + 1)
                    b, u = tiles[n_hg + 3][c]
                    dve.wait_ge(free[b], u + 1)
                    for h in range(HG):
                        o = hO3[:, c, h * P:(h + 1) * P]
                        dve.scalar_tensor_tensor(out=o, in0=o, scalar=rso[:, 4 * c + h:4 * c + h + 1],
                                                 in1=hSG3[:, c, h * P:(h + 1) * P], op0=ALU.mult,
                                                 op1=ALU.mult).then_inc(S["on_done"], 1)
                if k == "oaT":
                    for h in range(HG):
                        lo_scaled(oal3[:, h, :], BK[s][h], ghg[:, h:h + 1], oah3[:, h, :], "oah_done", h + 1)
                if k == "attn":
                    u = s[1]
                    bq, btp, bv = BK[s]
                    if u < NU:
                        i, h = units[u]
                        w = W_of(i)
                        wait_full(bq)
                        dve.wait_ge(S["bm_done"], u + 1)
                        if u >= 3:
                            wait_full(BK["attn", u - 1][1])
                        dve.tensor_tensor_reduce(tt[u % 3][:, 0:w], bank[bq[0]][:, 0:w], bm[u % 2][:, 0:w], -1.0,
                                                 3.4e38, ALU.add, ALU.min, nmx[:, u:u + 1]).then_inc(free[bq[0]], 1)
                    if bv is not None:
                        v = u - 3
                        i, h = units[v]
                        dve.wait_ge(S["e_done"], v + 1)
                        if v >= 2:
                            dve.wait_ge(free[7], BK["attn", v + 1][2][1] + 1)
                        dve.reciprocal(resum[:, v % 2:v % 2 + 1], esum[:, v:v + 1]).then_inc(S["rsum_done"], 1)
                        wait_full(bv)
                        dve.wait_ge(S["rsum_done"], v + 1)
                        dve.tensor_scalar(ob3[:, i, h * DH:(h + 1) * DH], bank[7][:, 0:DH], resum[:, v % 2:v % 2 + 1],
                                          None, ALU.mult).then_inc(free[7], 1)
                if k == "obT":
                    for q in range(4):
                        b, u = BK[s][q]
                        dve.wait_ge(S["obh_done"], q + 1)
                        dve.tensor_tensor(obl3[:, q, :], bank[b][:, :], obh3[:, q, :].bitcast(F32),
                                          ALU.subtract).then_inc(free[b], 1)

            for n in range(NPLAN):
                first = [s for s in side[n] if s[0] in ("mul", "put")]
                for s in first:
                    do_side(s)
                lo(n + AHEAD)
                if n in EARLY:
                    evict(n)
                for s in side[n]:
                    if s not in first:
                        do_side(s)
                if n not in EARLY:
                    evict(n)
            for q, k in enumerate(MLP_K):
                lo_scaled(hTl3[:, k, :], mlp_bank[k], vec[:, V_MLP + k:V_MLP + k + 1], hTh3[:, k, :], "hTh_done",
                          KD_ + q + 1)

            def final(t):
                dve.wait_ge(S["rf_done"], t + 1)
                for c in OUT_PARTS[t]:
                    dve.scalar_tensor_tensor(out=ys3[:, t, c], in0=y3[:, t, c], scalar=rsf[:, t:t + 1], in1=fg[:, c],
                                             op0=ALU.mult, op1=ALU.mult).then_inc(S["fin_done"], 1)

            def block_(it, last):
                for m in range(PER_FB):
                    if not (last and m + AHEAD >= PER_FB):
                        lo(NPLAN + m + AHEAD, it)
                    if m < 4:
                        dve.wait_ge(free[m], it * 2 + (MB + 1))
                        if m:
                            dve.wait_ge(S["hl_done"], it * 4 + m)
                        dve.tensor_tensor(hv[m % 2][:, :], rt[m % 2][:, :], rt[m % 2][:, :],
                                          ALU.mult).then_inc(S["hv_done"], 1)
                        dve.wait_ge(S["hh_done"], it * 4 + (m + 1))
                        dve.tensor_tensor(hl3[:, m, :], hv[m % 2][:, :], hh3[:, m, :].bitcast(F32),
                                          ALU.subtract).then_inc(S["hl_done"], 1)
                    if m in (5, 7):
                        half = (m - 5) // 2
                        if half == 0:
                            dve.wait_ge(S["hl_done"], it * 4 + 4)
                        for t in range(NT):
                            if half == 0:
                                b = 4 + t
                                dve.wait_ge(full[b], it + (MB2[t] + 1))
                            else:
                                b = t
                                dve.wait_ge(full[b], it * 2 + (MB + 2))
                            yy = y3[:, t, half * 512:(half + 1) * 512]
                            dve.scalar_tensor_tensor(out=yy, in0=bank[b][:, :], scalar=r2y[:, t:t + 1], in1=yy,
                                                     op0=ALU.mult, op1=ALU.add).then_inc(free[b], 1)
                            if last and half == 1 and t:
                                final(t - 1)

            dve.wait_ge(S["ry_done"], 1)
            dve.wait_ge(fg_in, 16)
            loop_blocks(dve, block_)
            final(NT - 1)

        @block.tensor
        def _(pe):
            def wait_free(bu):
                if bu[1]:
                    pe.wait_ge(free[bu[0]], bu[1])

            def three(dst, lh, ll, rh, rl, start, stop):
                pe.matmul(dst, lh, rh, start=start, stop=False)
                pe.matmul(dst, lh, rl, start=False, stop=False)
                return pe.matmul(dst, ll, rh, start=False, stop=stop)

            def transposes(dst_bu, srcs):
                wait_free(dst_bu)
                for q, src in enumerate(srcs):
                    last = pe.transpose(bank[dst_bu[0]][:, q * P:(q + 1) * P], src, ident)
                last.then_inc(full[dst_bu[0]], 1)

            pe.wait_ge(ident_in, 16)
            for t in range(NT):
                pe.wait_ge(S["xn_done"], t + 1)
                for k in range(KD_):
                    ins = pe.transpose(bank[k][:, t * P:(t + 1) * P], xs3[:, t, k * P:(k + 1) * P], ident)
                    if t == NT - 1:
                        ins.then_inc(full[k], 1)

            def token_slab(n, hi_, lo_, ts, k0, first, last):
                s = n % SLOTS
                wh, wl = slab_view(whi, s, 2), slab_view(wlo, s, 2)
                for t, kk in [(t, kk) for t in range(NT) for kk in range(2)]:
                    b, u = ts[t]
                    st, sp_ = first and kk == 0, last and kk == 1
                    if st:
                        wait_free((b, u))
                    k = k0 + kk
                    ins = three(bank[b][:, :], hi_[:, k, t * P:(t + 1) * P], lo_[:, k, t * P:(t + 1) * P],
                                wh[:, kk, :], wl[:, kk, :], st, sp_)
                    if sp_:
                        ins.then_inc(full[b], 1)
                return ins

            def feature_tile(bu, hi_, lo_, wh, wl, kt, c0, split_of=None):
                b = bu[0]
                wait_free(bu)
                for k in range(kt):
                    if split_of is not None:
                        pe.wait_ge(free[split_of[k][0]], split_of[k][1] + 1)
                    ins = three(bank[b][:, :], wh[:, k, c0:c0 + P], wl[:, k, c0:c0 + P], hi_[:, k, :], lo_[:, k, :],
                                k == 0, k == kt - 1)
                return ins.then_inc(full[b], 1)

            def mms(n):
                kind, j = PLAN[n]
                s = n % SLOTS
                pe.wait_ge(lo_done, n + 1)
                if kind in ("c0", "hi", "hg"):
                    ins = token_slab(n, hTh3, hTl3, tiles[n], 2 * j, j == 0, j == 3)
                elif kind == "c1":
                    b, u = c1_bank
                    wait_free(c1_bank)
                    wh = whi[s][:, 0:KD_ * (DH + IH)].rearrange("p (k c) -> p k c", k=KD_)
                    wl = wlo[s][:, 0:KD_ * (DH + IH)].rearrange("p (k c) -> p k c", k=KD_)
                    for k in range(KD_):
                        ins = three(bank[b][0:DH + IH, :], wh[:, k, :], wl[:, k, :], hTh3[:, k, :], hTl3[:, k, :],
                                    k == 0, k == KD_ - 1)
                    ins.then_inc(full[b], 1)
                elif kind in ("hf", "hq", "ga", "gb"):
                    ins = feature_tile(tiles[n][0], hTh3, hTl3, slab_view(whi, s, KD_), slab_view(wlo, s, KD_), KD_, 0,
                                       [(k, 0) for k in range(KD_)] if n == 0 else None)
                elif kind in ("iq", "uq"):
                    split_of = BK["cqT",] if kind == "iq" else None
                    for q in range(4):
                        ins = feature_tile(tiles[n][q], cqh3, cql3, slab_view(whi, s, 2), slab_view(wlo, s, 2), 2, q * P,
                                           split_of if q == 0 else None)
                elif kind in ("ua", "ub"):
                    h_, l_ = (oah3, oal3) if kind == "ua" else (obh3, obl3)
                    split_of = BK["oaT" if kind == "ua" else "obT",] if j == 0 else None
                    for q in range(2):
                        ins = feature_tile(tiles[n][q], h_, l_, slab_view(whi, s, 4), slab_view(wlo, s, 4), 4, q * P,
                                           split_of if q == 0 else None)
                elif kind == "wo":
                    if j < 4:
                        pe.wait_ge(S["mxl_done"], 2 * j + 2)
                    ins = token_slab(n, mxh3, mxl3, tiles[n], 2 * (j % 4), j % 4 == 0, j % 4 == 3)
                if n in by_count:
                    ins.then_inc(slab_used, 1)

            def do_side(s):
                k = s[0]
                if k == "bias_rows":
                    pe.wait_ge(const_in, 48)
                    b, u = BK[s][0]
                    wait_free((b, u))
                    pe.matmul(bank[b][0:AH, 0:BT_LEN], rb[:, :], oneh[:, :], start=True, stop=True).then_inc(full[b], 1)
                if k == "ikT":
                    b, u = BK[s][0]
                    pe.wait_ge(free[c1_bank[0]], c1_bank[1] + 1)
                    wait_free((b, u))
                    w = DH + IH
                    for t in range(NT):
                        ins = pe.transpose(bank[b][:, t * w:(t + 1) * w], ikT[:, t * P:(t + 1) * P], ident[0:w, 0:w])
                    ins.then_inc(full[b], 1)
                if k == "cqT":
                    pe.wait_ge(S["cqn_done"], NT)
                    for q in range(2):
                        transposes(BK[s][q], [c03[:, t, q * P:(q + 1) * P] for t in range(NT)])
                if k == "kdT":
                    pe.wait_ge(S["kd_done"], GR)
                    for g in range(GR):
                        transposes(BK[s][g], [kd5[:, t, g].rearrange("p u d -> p (u d)") for t in range(NT)])
                    pe.wait_ge(S["ikn_done"], NT)
                    transposes(BK[s][2], [ikn4[:, t].rearrange("p u d -> p (u d)") for t in range(NT)])
                if k == "index":
                    _, u, i, h = s
                    b, n_ = BK[s][0]
                    if u == 0:
                        for q in range(4):
                            b_, u_ = tiles[n_iq][q]
                            pe.wait_ge(free[b_], u_ + 1)
                        b_, u_ = BK["kdT",][2]
                        pe.wait_ge(free[b_], u_ + 1)
                    wait_free((b, n_))
                    r_ = heads_rows(h)
                    pe.matmul(bank[b][:, 0:W_of(i)], iq3[r_, h // 2, i * P:(i + 1) * P], ikd[r_, 0:W_of(i)],
                              start=True, stop=True).then_inc(full[b], 1)
                if k == "mul":
                    l = s[1]
                    B, H = 2 << l, 1 << l
                    pe.wait_ge(S["xm_done"], 2 * (l + 1))
                    xu = hX[l % 2][:, :].rearrange("p (u t) -> p u t", t=C)
                    for q, bu in enumerate(BK[s]):
                        wait_free(bu)
                        for v in range(8):
                            un = xu[:, 8 * q + v, :]
                            rhs = un.rearrange("p (n b) -> p n b", b=B)[:, :, H:B]
                            ins = pe.matmul(bank[bu[0]][:, 64 * v:64 * v + 64].rearrange("p (n h) -> p n h", h=H), un, rhs,
                                            start=True, stop=True)
                        ins.then_inc(full[bu[0]], 1)
                if k == "diag":
                    for q, bu in enumerate(BK[s]):
                        wait_free(bu)
                        for v in range(4):
                            un = 4 * q + v
                            ins = pe.matmul(bank[bu[0]][:, v * P:(v + 1) * P], hk_u[:, un, :], hq_u[:, un, :],
                                            start=True, stop=True)
                        ins.then_inc(full[bu[0]], 1)
                if k == "kT":
                    c = s[1]
                    if c == 0:
                        pe.wait_ge(S["kk_done"], 1)
                    transposes(BK[s][0], [hk_u[:, h * NT + c, :] for h in range(HG)])
                if k == "state":
                    c = s[1]
                    bs = BK[s][0]
                    b, u = BK["kT", c][0]
                    pe.wait_ge(free[b], u + 1)
                    if c == 0:
                        for b, u in tiles[n_hi + 3]:
                            pe.wait_ge(free[b], u + 1)
                    wait_free(bs)
                    for h in range(HG):
                        ins = pe.matmul(bank[bs[0]][:, h * P:(h + 1) * P], hKT[:, h * P:(h + 1) * P],
                                        hV3[:, c, h * P:(h + 1) * P], start=True, stop=True)
                    ins.then_inc(full[bs[0]], 1)
                if k == "out":
                    c = s[1]
                    bo = BK[s][0]
                    if c == 0:
                        pe.wait_ge(S["qd_done"], 1)
                        for b, u in BK["mul", LEVELS - 1]:
                            pe.wait_ge(free[b], u + 1)
                    else:
                        b, u = BK["state", c - 1][0]
                        pe.wait_ge(free[b], u + 1)
                    wait_free(bo)
                    for h in range(HG):
                        un = h * NT + c
                        dst = bank[bo[0]][:, h * P:(h + 1) * P]
                        ins = pe.matmul(dst, ha_u[:, un, :], hV3[:, c, h * P:(h + 1) * P], start=True, stop=c == 0)
                        if c:
                            ins = pe.matmul(dst, hq_u[:, un, :], hS[:, h * P:(h + 1) * P], start=False, stop=True)
                    ins.then_inc(full[bo[0]], 1)
                if k == "oaT":
                    pe.wait_ge(S["on_done"], 16)
                    for h in range(HG):
                        transposes(BK[s][h], [hO3[:, t, h * P:(h + 1) * P] for t in range(NT)])
                if k == "flip":
                    h = s[1]
                    b, u = BK[s][0]
                    pe.wait_ge(S["bt_in"], 16)
                    wait_free((b, u))
                    pe.matmul(bank[b][:, :], flip, bt[:, 512 * h:512 * h + 512], start=True, stop=True).then_inc(full[b], 1)
                if k == "attn":
                    u = s[1]
                    bq, btp, bv = BK[s]
                    if u < NU:
                        i, h = units[u]
                        if u == 0:
                            for q in range(4):
                                b_, u_ = tiles[n_uq][q]
                                pe.wait_ge(free[b_], u_ + 1)
                            for q in range(GR):
                                b_, u_ = BK["kdT",][q]
                                pe.wait_ge(free[b_], u_ + 1)
                        wait_free(bq)
                        r_ = heads_rows(h)
                        pe.matmul(bank[bq[0]][:, 0:W_of(i)], aq3[r_, h // 2, i * P:(i + 1) * P],
                                  kdup3[r_, h // 4, 0:W_of(i)], start=True, stop=True).then_inc(full[bq[0]], 1)
                    if btp is not None:
                        v = u - 2
                        i, h = units[v]
                        pe.wait_ge(S["e_done"], v + 1)
                        transposes(btp, [tt[v % 3][:, q * P:(q + 1) * P] for q in range(i + 1)])
                    if bv is not None:
                        v = u - 3
                        i, h = units[v]
                        b6 = BK["attn", v + 2][1]
                        pe.wait_ge(free[6], b6[1] + 1)
                        wait_free(bv)
                        g = h // 4
                        for q in range(i + 1):
                            ins = pe.matmul(bank[7][:, 0:DH], et[v % 2][:, q * P:(q + 1) * P],
                                            c03[:, q, QL + GR * DH + g * DH:QL + GR * DH + (g + 1) * DH],
                                            start=q == 0, stop=q == i)
                        ins.then_inc(full[7], 1)
                if k == "obT":
                    pe.wait_ge(free[7], BK["attn", NU + 2][2][1] + 1)
                    for q in range(4):
                        transposes(BK[s][q], [ob3[:, t, q * P:(q + 1) * P] for t in range(NT)])

            for n in range(NPLAN):
                mms(n)
                for s in side[n]:
                    do_side(s)


            for k in MLP_K[0:5]:
                wait_free(mlp_bank[k])
            for t in range(NT):
                b, u = tiles[n_wo + 7][t]
                pe.wait_ge(free[b], u + 1)
                for k in MLP_K[0:5]:
                    ins = pe.transpose(bank[k][:, t * P:(t + 1) * P], y3[:, t, k * P:(k + 1) * P], ident)
                    if t == NT - 1:
                        ins.then_inc(full[k], 1)
            for k in MLP_K[5:8]:
                transposes(mlp_bank[k], [y3[:, t, k * P:(k + 1) * P] for t in range(NT)])

            def block_(it, last):
                for m in range(PER_FB):
                    n = NPLAN + m
                    s = n % SLOTS
                    pe.wait_ge(lo_done, it * PER_FB + (n + 1))
                    if m < 4:
                        wh, wl = slab_view(whi, s, KD_), slab_view(wlo, s, KD_)
                        pe.wait_ge(free[m], it * 2 + MB)
                        for q, k in enumerate(MLP_K):
                            if m == 0:
                                pe.wait_ge(free[k], mlp_bank[k][1] + 1)
                            ins = three(bank[m][:, :], wh[:, k, :], wl[:, k, :], hTh3[:, k, :], hTl3[:, k, :],
                                        q == 0, q == KD_ - 1)
                        ins.then_inc(full[m], 1)
                    else:
                        wh, wl = slab_view(whi, s, 2), slab_view(wlo, s, 2)
                        first, k0 = m % 2 == 0, 2 * (m % 2)
                        for t in range(NT):
                            for kk in range(2):
                                k = k0 + kk
                                if m < 6 and t == 0:
                                    pe.wait_ge(S["hl_done"], it * 4 + (k + 1))
                                b = 4 + t if m < 6 else t
                                if first and kk == 0:
                                    pe.wait_ge(free[b], it + MB2[t] if m < 6 else it * 2 + (MB + 1))
                                ins = three(bank[b][:, :], hh3[:, k, t * P:(t + 1) * P], hl3[:, k, t * P:(t + 1) * P],
                                            wh[:, kk, :], wl[:, kk, :], first and kk == 0, k == 3)
                                if k == 3:
                                    ins.then_inc(full[b], 1)
                        if first:
                            ins.then_inc(slab_used, 1)

            loop_blocks(pe, block_)


def constants():
    p = np.arange(P)
    k = np.zeros((P, K_COLS), np.float32)
    k[:, K_IDENT:K_IDENT + P] = np.eye(P)
    for l in range(LEVELS):
        half, width = 1 << l, 2 << l
        t = np.arange(P)
        right = t[t % width >= half]
        same = (p[:, None] // width == right[None, :] // width) & (p[:, None] % width < half)
        k[:, K_MASK + 64 * l:K_MASK + 64 * l + 64] = same
    k[:, K_RESET:K_RESET + T] = (np.arange(T) % C != 0)
    k[:, K_CAUSAL:K_CAUSAL + P] = np.where(p[None, :] <= p[:, None], 0.0, NEG)
    k[:, K_FLIP:K_FLIP + P] = np.eye(P)[::-1]
    dist = np.maximum(WIN - 1 - np.arange(BT_LEN), 0)
    exact, reach = BUCKETS // 2, 128
    large = exact + (np.log(np.maximum(dist, 1).astype(np.float32) / exact) / np.log(reach / exact)
                     * (BUCKETS - exact)).astype(np.int32)
    bucket = np.where(dist < exact, dist, np.minimum(large, BUCKETS - 1))
    onehot = (bucket[None, :] == np.arange(BUCKETS)[:, None]).astype(np.float32)
    return k, onehot


def kernel(x, attn_norm_g, w_in, hgrn_lb_logits, hgrn_norm_g, w_up_hgrn, q_norm_g, w_uq, w_iq, idx_k_norm_g,
           idx_k_norm_b, rel_bias, w_up_attn, w_o, mlp_norm_g, w_mlp_in, w_mlp_out, final_norm_g):
    import concourse.bacc as _bacc
    from concourse.bass_utils import run_bass_kernel_spmd as _run

    A = np.ascontiguousarray

    def slab(w):
        k, c = w.shape[0] // P, w.shape[1]
        s = np.asarray(w).reshape(k, P, c).transpose(1, 0, 2).reshape(P, k * c)
        return s if k * c == SLAB else np.pad(s, ((0, 0), (0, SLAB - k * c)))

    wi = np.asarray(w_in)[0]
    widths = (HGW, HGW, HGW, HGW, QL, GR * DH, GR * DH, DH, IH, D, D)
    o = np.cumsum((0,) + widths)
    q0, f0, i0, g0, c0, ik0, ga0, gb0 = o[0], o[1], o[2], o[3], o[4], o[7], o[9], o[10]
    up_h, up_a, wo = (np.asarray(w)[0] for w in (w_up_hgrn, w_up_attn, w_o))
    uq, iq = np.asarray(w_uq)[0], np.asarray(w_iq)[0]
    m_in, m_out = np.asarray(w_mlp_in)[0], np.asarray(w_mlp_out)[0]
    by_token = {"c0": c0, "hi": i0, "hg": g0}
    by_feature = {"hf": f0, "hq": q0, "ga": ga0, "gb": gb0}
    parts = []
    for kind, j in PLAN:
        if kind in by_token:
            parts.append(wi[2 * P * j:2 * P * (j + 1), by_token[kind]:by_token[kind] + 512])
        elif kind in by_feature:
            parts.append(wi[:, by_feature[kind] + P * j:by_feature[kind] + P * (j + 1)])
        elif kind == "c1":
            parts.append(wi[:, ik0:ik0 + DH + IH])
        elif kind in ("iq", "uq"):
            parts.append(iq if kind == "iq" else uq)
        elif kind in ("ua", "ub"):
            parts.append((up_h if kind == "ua" else up_a)[:, 2 * P * j:2 * P * (j + 1)])
        else:
            parts.append(wo[2 * P * (j % 4):2 * P * (j % 4 + 1), 512 * (j // 4):512 * (j // 4 + 1)])
    for f in range(0, F, FB):
        parts += [m_in[:, f + P * j:f + P * (j + 1)] for j in range(4)]
        parts += [m_out[f + 2 * P * j:f + 2 * P * (j + 1), 512 * h:512 * (h + 1)] for h in range(2) for j in range(2)]
    slabs = A(np.stack([slab(w) for w in parts]))

    def cols(v):
        return np.asarray(v).reshape(-1, P).T

    lbl = np.asarray(hgrn_lb_logits)
    two = lambda v: np.concatenate([np.asarray(v)[0]] * 2).reshape(1, P).T
    vecs = A(np.concatenate([cols(attn_norm_g), cols(mlp_norm_g), cols(q_norm_g), cols(hgrn_norm_g), cols(lbl[0]),
                             cols(lbl[1]), two(idx_k_norm_g), two(idx_k_norm_b)], axis=1))
    k, onehot = constants()
    arrays = {"x": A(np.asarray(x)), "slabs": slabs, "vecs": vecs, "consts": k, "onehot": onehot,
              "rel_bias": A(np.asarray(rel_bias)), "final_g": A(np.asarray(final_norm_g))}
    nc = _bacc.Bacc("TRN2", target_bir_lowering=False, num_devices=1)
    args = [nc.dram_tensor(n, a.shape, mybir.dt.from_np(a.dtype), kind="ExternalInput").ap() for n, a in arrays.items()]
    out = nc.dram_tensor("out", (1, T, D), F32, kind="ExternalOutput").ap()
    build(nc, *args, out)
    r = _run(nc, [arrays], core_ids=[0])
    return r.results[0]["out"]
```
